# Optimizing a Trainium2 kernel written in Bass

```python
import math
import jax, jax.numpy as jnp
from jax import lax
import numpy as np

D_MODEL = 1024
BATCH = 1
SEQ = 256
DEPTH = 4

N_MIXERS = 3
N_A = (DEPTH + 2) // 3
N_B = (DEPTH + 1) // 3
N_C = DEPTH // 3
EPS = 1e-6
CONV_W = 4
N_MEM = 256

M_D_INNER = 2 * D_MODEL
M_HEAD_DIM = 64
M_HEADS = M_D_INNER // M_HEAD_DIM
M_GROUPS = 8
M_STATE = 128
M_CONV_DIM = M_D_INNER + 2 * M_GROUPS * M_STATE
M_IN = M_D_INNER + M_CONV_DIM + M_HEADS
SSD_CHUNK = 64
DT_MIN = 1e-3
DT_MAX = 1e-1

H_EXPAND = 128
H_HEADS = D_MODEL // H_EXPAND
H_DV = D_MODEL // H_HEADS
HGRN_CHUNK = 32

G_HEAD_DIM = 128
G_QK_HEADS = D_MODEL // G_HEAD_DIM
G_V_HEADS = 2 * G_QK_HEADS
G_KEY_DIM = G_QK_HEADS * G_HEAD_DIM
G_VAL_DIM = G_V_HEADS * G_HEAD_DIM
G_CONV_DIM = 2 * G_KEY_DIM + G_VAL_DIM
G_IN = G_CONV_DIM + G_VAL_DIM + 2 * G_V_HEADS
GDN_CHUNK = 64

X_HEADS = 4
X_HEAD_DIM = D_MODEL // X_HEADS

D_FF = 2816
FFN_CONV_W = 3


def rmsnorm(x, w):
    x32 = x.astype(jnp.float32)
    y = x32 * lax.rsqrt(jnp.mean(x32 * x32, axis=-1, keepdims=True) + EPS)
    return (y * w.astype(jnp.float32)).astype(x.dtype)

def l2norm(x):
    x32 = x.astype(jnp.float32)
    return x32 * lax.rsqrt(jnp.sum(x32 * x32, axis=-1, keepdims=True) + EPS)

def causal_dwconv(x, w):
    width, ch = w.shape
    return lax.conv_general_dilated(x, w[:, None, :].astype(x.dtype), window_strides=(1,),
                                    padding=[(width - 1, 0)],
                                    dimension_numbers=('NWC', 'WIO', 'NWC'),
                                    feature_group_count=ch)

def ssd_chunk(x, dt, a, bm, cm, chunk):
    bsz, seq, nh, p = x.shape
    ng, ns = bm.shape[2], bm.shape[3]
    r = nh // ng
    nc = seq // chunk
    f32 = jnp.float32
    xc = (x * dt[..., None]).astype(f32).reshape(bsz, nc, chunk, ng, r, p)
    acum = jnp.cumsum((dt * a).astype(f32).reshape(bsz, nc, chunk, ng, r), axis=2)
    bc = bm.astype(f32).reshape(bsz, nc, chunk, ng, ns)
    cc = cm.astype(f32).reshape(bsz, nc, chunk, ng, ns)
    causal = jnp.tril(jnp.ones((chunk, chunk), dtype=bool))[:, :, None, None]
    decay = jnp.exp(jnp.where(causal, acum[:, :, :, None] - acum[:, :, None, :], -jnp.inf))
    cb = jnp.einsum('bnlgk,bnsgk->bnlsg', cc, bc)
    y_diag = jnp.einsum('bnlsgr,bnsgrp->bnlgrp', cb[..., None] * decay, xc)

    def step(state, inp):
        c_, b_, x_, ac_ = inp
        y = jnp.einsum('blgk,bgrpk->blgrp', c_, state) * jnp.exp(ac_)[..., None]
        last = ac_[:, -1]
        ds = jnp.einsum('bsgk,bsgrp->bgrpk', b_, x_ * jnp.exp(last[:, None] - ac_)[..., None])
        state = state * jnp.exp(last)[..., None, None] + ds
        return state, y

    s0 = jnp.zeros((bsz, ng, r, p, ns), f32)
    xs = tuple(jnp.moveaxis(t, 1, 0) for t in (cc, bc, xc, acum))
    _, y_off = lax.scan(step, s0, xs)
    return (y_diag + jnp.moveaxis(y_off, 0, 1)).reshape(bsz, seq, nh, p)

def gla_chunk(q, k, v, log_f, chunk):
    bsz, seq, nh, dk = q.shape
    nc = seq // chunk

    def blocks(t):
        return t.astype(jnp.float32).reshape(bsz, nc, chunk, nh, t.shape[-1]).transpose(0, 1, 3, 2, 4)

    q, k, v = blocks(q), blocks(k), blocks(v)
    gc = jnp.cumsum(blocks(log_f), axis=3)
    g_last = gc[:, :, :, -1]
    q_dec = q * jnp.exp(gc)
    k_inv = k * jnp.exp(-gc)
    k_end = k * jnp.exp(g_last[:, :, :, None] - gc)
    causal = jnp.tril(jnp.ones((chunk, chunk), dtype=bool))
    att = jnp.where(causal, jnp.einsum('bnhlk,bnhsk->bnhls', q_dec, k_inv), 0.0)
    o_intra = jnp.einsum('bnhls,bnhsv->bnhlv', att, v)

    def step(state, inp):
        qd, ke, vv, gl = inp
        o = jnp.einsum('bhlk,bhkv->bhlv', qd, state)
        state = state * jnp.exp(gl)[..., None] + jnp.einsum('bhsk,bhsv->bhkv', ke, vv)
        return state, o

    s0 = jnp.zeros((bsz, nh, dk, v.shape[-1]), jnp.float32)
    xs = tuple(jnp.moveaxis(t, 1, 0) for t in (q_dec, k_end, v, g_last))
    _, o_inter = lax.scan(step, s0, xs)
    o = o_intra + jnp.moveaxis(o_inter, 0, 1)
    return o.transpose(0, 1, 3, 2, 4).reshape(bsz, seq, nh, -1)

def gated_delta_chunk(q, k, v, g, beta, chunk):
    bsz, seq, nh, dk = q.shape
    dv = v.shape[-1]
    nc = seq // chunk

    def blocks(t):
        return t.astype(jnp.float32).reshape(bsz, nc, chunk, nh, t.shape[-1]).transpose(0, 1, 3, 2, 4)

    def blocks_s(t):
        return t.astype(jnp.float32).reshape(bsz, nc, chunk, nh).transpose(0, 1, 3, 2)

    q, k, v = blocks(q), blocks(k), blocks(v)
    beta = blocks_s(beta)
    gc = jnp.cumsum(blocks_s(g), axis=-1)
    incl = jnp.tril(jnp.ones((chunk, chunk), dtype=bool))
    strict = jnp.tril(jnp.ones((chunk, chunk), dtype=bool), k=-1)
    decay = jnp.exp(jnp.where(incl, gc[..., :, None] - gc[..., None, :], -jnp.inf))
    kb = k * beta[..., None]
    m = jnp.where(strict, jnp.einsum('bnhlk,bnhsk->bnhls', kb, k) * decay, 0.0)
    a_mat = m + jnp.eye(chunk, dtype=jnp.float32)
    rhs = jnp.concatenate([v * beta[..., None], kb * jnp.exp(gc)[..., None]], axis=-1)
    sol = lax.linalg.triangular_solve(a_mat, rhs, left_side=True, lower=True, unit_diagonal=True)
    u, w = sol[..., :dv], sol[..., dv:]
    att = jnp.einsum('bnhlk,bnhsk->bnhls', q, k) * decay
    q_dec = q * jnp.exp(gc)[..., None]
    g_last = gc[..., -1]
    k_end = k * jnp.exp(g_last[..., None] - gc)[..., None]

    def step(state, inp):
        qd, aa, uu, ww, ke, gl = inp
        v_new = uu - jnp.einsum('bhlk,bhkv->bhlv', ww, state)
        o = jnp.einsum('bhlk,bhkv->bhlv', qd, state) + jnp.einsum('bhls,bhsv->bhlv', aa, v_new)
        state = state * jnp.exp(gl)[..., None, None] + jnp.einsum('bhsk,bhsv->bhkv', ke, v_new)
        return state, o

    s0 = jnp.zeros((bsz, nh, dk, dv), jnp.float32)
    xs = tuple(jnp.moveaxis(t, 1, 0) for t in (q_dec, att, u, w, k_end, g_last))
    _, o = lax.scan(step, s0, xs)
    o = jnp.moveaxis(o, 0, 1)
    return o.transpose(0, 1, 3, 2, 4).reshape(bsz, seq, nh, dv)

def mamba2_mixer(h, in_w, conv_w, conv_b, dt_bias, a_log, d_skip, norm_w, out_w):
    bsz, seq, _ = h.shape
    f32 = jnp.float32
    proj = h @ in_w
    z = proj[..., :M_D_INNER]
    xbc = jax.nn.silu(causal_dwconv(proj[..., M_D_INNER:M_D_INNER + M_CONV_DIM], conv_w) + conv_b)
    dt = jax.nn.softplus(proj[..., M_D_INNER + M_CONV_DIM:].astype(f32) + dt_bias.astype(f32))
    xs = xbc[..., :M_D_INNER].reshape(bsz, seq, M_HEADS, M_HEAD_DIM)
    bm = xbc[..., M_D_INNER:M_D_INNER + M_GROUPS * M_STATE].reshape(bsz, seq, M_GROUPS, M_STATE)
    cm = xbc[..., M_D_INNER + M_GROUPS * M_STATE:].reshape(bsz, seq, M_GROUPS, M_STATE)
    a = -jnp.exp(a_log.astype(f32))
    y = ssd_chunk(xs, dt, a, bm, cm, SSD_CHUNK) + d_skip.astype(f32)[:, None] * xs.astype(f32)
    y = y.reshape(bsz, seq, M_D_INNER).astype(h.dtype) * jax.nn.silu(z)
    gs = M_D_INNER // M_GROUPS
    y = rmsnorm(y.reshape(bsz, seq, M_GROUPS, gs), norm_w.reshape(M_GROUPS, gs))
    return y.reshape(bsz, seq, M_D_INNER) @ out_w

def hgrn2_mixer(h, in_w, lower_bound, norm_w, out_w):
    bsz, seq, _ = h.shape
    q, f, i, g = jnp.split(h @ in_w, 4, axis=-1)

    def heads(t):
        return t.reshape(bsz, seq, H_HEADS, -1)

    lb = lower_bound.astype(jnp.float32)
    forget = lb + (1.0 - lb) * jax.nn.sigmoid(f.astype(jnp.float32))
    o = gla_chunk(heads(jax.nn.silu(q)) * H_EXPAND ** -0.5, heads(1.0 - forget), heads(i),
                  heads(jnp.log(forget)), HGRN_CHUNK)
    o = rmsnorm(o.astype(h.dtype), norm_w) * jax.nn.silu(heads(g))
    return o.reshape(bsz, seq, D_MODEL) @ out_w

def gated_deltanet_mixer(h, in_w, conv_w, a_log, dt_bias, norm_w, out_w):
    bsz, seq, _ = h.shape
    f32 = jnp.float32
    proj = h @ in_w
    qkv = jax.nn.silu(causal_dwconv(proj[..., :G_CONV_DIM], conv_w))
    z = proj[..., G_CONV_DIM:G_CONV_DIM + G_VAL_DIM]
    b = proj[..., G_CONV_DIM + G_VAL_DIM:G_CONV_DIM + G_VAL_DIM + G_V_HEADS]
    a = proj[..., G_CONV_DIM + G_VAL_DIM + G_V_HEADS:]
    q = l2norm(qkv[..., :G_KEY_DIM].reshape(bsz, seq, G_QK_HEADS, G_HEAD_DIM))
    k = l2norm(qkv[..., G_KEY_DIM:2 * G_KEY_DIM].reshape(bsz, seq, G_QK_HEADS, G_HEAD_DIM))
    v = qkv[..., 2 * G_KEY_DIM:].reshape(bsz, seq, G_V_HEADS, G_HEAD_DIM)
    rep = G_V_HEADS // G_QK_HEADS
    q = jnp.repeat(q, rep, axis=2) * G_HEAD_DIM ** -0.5
    k = jnp.repeat(k, rep, axis=2)
    beta = jax.nn.sigmoid(b.astype(f32))
    g = -jnp.exp(a_log.astype(f32)) * jax.nn.softplus(a.astype(f32) + dt_bias.astype(f32))
    o = gated_delta_chunk(q, k, v, g, beta, GDN_CHUNK)
    o = rmsnorm(o.astype(h.dtype), norm_w) * jax.nn.silu(z.reshape(bsz, seq, G_V_HEADS, G_HEAD_DIM))
    return o.reshape(bsz, seq, G_VAL_DIM) @ out_w

def memory_cross_attention(h, mem_n, wq, wkv, wo):
    bsz, seq, _ = h.shape
    q = (h @ wq).reshape(bsz, seq, X_HEADS, X_HEAD_DIM)
    k, v = jnp.split(mem_n @ wkv, 2, axis=-1)
    k = k.reshape(bsz, -1, X_HEADS, X_HEAD_DIM)
    v = v.reshape(bsz, -1, X_HEADS, X_HEAD_DIM)
    s = jnp.einsum('blhd,bmhd->bhlm', q, k).astype(jnp.float32) * X_HEAD_DIM ** -0.5
    p = jax.nn.softmax(s, axis=-1).astype(h.dtype)
    o = jnp.einsum('bhlm,bmhd->blhd', p, v).reshape(bsz, seq, D_MODEL)
    return o @ wo

def conv_glu_ffn(h, up_w, conv_w, conv_b, down_w):
    gate, up = jnp.split(h @ up_w, 2, axis=-1)
    gate = causal_dwconv(gate, conv_w) + conv_b
    return (jax.nn.silu(gate) * up) @ down_w

def first_inputs(seed: int = 0) -> dict:
    key = jax.random.key(seed)
    keys = iter(jax.random.split(key, 48))
    d = D_MODEL
    out_scale = (2 * DEPTH) ** -0.5

    def normal(shape, scale):
        return scale * jax.random.normal(next(keys), shape, jnp.float32)

    def gain(shape):
        return 1.0 + 0.05 * jax.random.normal(next(keys), shape, jnp.float32)

    def dt_bias(shape):
        u = jax.random.uniform(next(keys), shape, jnp.float32)
        dt = jnp.exp(u * (math.log(DT_MAX) - math.log(DT_MIN)) + math.log(DT_MIN))
        return dt + jnp.log(-jnp.expm1(-dt))

    def a_log(shape):
        return jnp.log(jax.random.uniform(next(keys), shape, jnp.float32, 1.0, 16.0))

    return {
        'x': normal((BATCH, SEQ, d), 1.0),
        'mem': normal((BATCH, N_MEM, d), 1.0),
        'ln_mix': gain((DEPTH, d)),
        'ln_xattn': gain((DEPTH, d)),
        'ln_mem': gain((DEPTH, d)),
        'ln_ffn': gain((DEPTH, d)),
        'final_norm': gain((d,)),
        'm_in_w': normal((N_A, d, M_IN), d ** -0.5),
        'm_conv_w': normal((N_A, CONV_W, M_CONV_DIM), CONV_W ** -0.5),
        'm_conv_b': normal((N_A, M_CONV_DIM), 0.02),
        'm_dt_bias': dt_bias((N_A, M_HEADS)),
        'm_a_log': a_log((N_A, M_HEADS)),
        'm_d': gain((N_A, M_HEADS)),
        'm_norm_w': gain((N_A, M_D_INNER)),
        'm_out_w': normal((N_A, M_D_INNER, d), M_D_INNER ** -0.5 * out_scale),
        'h_in_w': normal((N_B, d, 4 * d), d ** -0.5),
        'h_lower_bounds': normal((DEPTH, d), 0.1),
        'h_norm_w': gain((N_B, H_DV)),
        'h_out_w': normal((N_B, d, d), d ** -0.5 * out_scale),
        'g_in_w': normal((N_C, d, G_IN), d ** -0.5),
        'g_conv_w': normal((N_C, CONV_W, G_CONV_DIM), CONV_W ** -0.5),
        'g_a_log': a_log((N_C, G_V_HEADS)),
        'g_dt_bias': dt_bias((N_C, G_V_HEADS)),
        'g_norm_w': gain((N_C, G_HEAD_DIM)),
        'g_out_w': normal((N_C, G_VAL_DIM, d), G_VAL_DIM ** -0.5 * out_scale),
        'xa_q': normal((DEPTH, d, d), d ** -0.5),
        'xa_kv': normal((DEPTH, d, 2 * d), d ** -0.5),
        'xa_o': normal((DEPTH, d, d), d ** -0.5 * out_scale),
        'f_up': normal((DEPTH, d, 2 * D_FF), d ** -0.5),
        'f_conv_w': normal((DEPTH, FFN_CONV_W, D_FF), FFN_CONV_W ** -0.5),
        'f_conv_b': normal((DEPTH, D_FF), 0.02),
        'f_down': normal((DEPTH, D_FF, d), D_FF ** -0.5 * out_scale),
    }

def first_block(x, mem, ln_mix, ln_xattn, ln_mem, ln_ffn, final_norm,
              m_in_w, m_conv_w, m_conv_b, m_dt_bias, m_a_log, m_d, m_norm_w, m_out_w,
              h_in_w, h_lower_bounds, h_norm_w, h_out_w,
              g_in_w, g_conv_w, g_a_log, g_dt_bias, g_norm_w, g_out_w,
              xa_q, xa_kv, xa_o, f_up, f_conv_w, f_conv_b, f_down):
    lb = jnp.cumsum(jax.nn.softmax(h_lower_bounds.astype(jnp.float32), axis=0), axis=0)
    lb = lb - lb[:1]
    ia = 0
    ib = 0
    ic = 0
    for i in range(DEPTH):
        hn = rmsnorm(x, ln_mix[i])
        if i % N_MIXERS == 0:
            mix = mamba2_mixer(hn, m_in_w[ia], m_conv_w[ia], m_conv_b[ia], m_dt_bias[ia],
                               m_a_log[ia], m_d[ia], m_norm_w[ia], m_out_w[ia])
            ia += 1
        elif i % N_MIXERS == 1:
            mix = hgrn2_mixer(hn, h_in_w[ib], lb[i], h_norm_w[ib], h_out_w[ib])
            ib += 1
        else:
            mix = gated_deltanet_mixer(hn, g_in_w[ic], g_conv_w[ic], g_a_log[ic], g_dt_bias[ic],
                                       g_norm_w[ic], g_out_w[ic])
            ic += 1
        x = x + mix.astype(x.dtype)
        x = x + memory_cross_attention(rmsnorm(x, ln_xattn[i]), rmsnorm(mem, ln_mem[i]),
                                       xa_q[i], xa_kv[i], xa_o[i]).astype(x.dtype)
        x = x + conv_glu_ffn(rmsnorm(x, ln_ffn[i]), f_up[i], f_conv_w[i], f_conv_b[i],
                             f_down[i]).astype(x.dtype)
    return rmsnorm(x, final_norm)


DEPTH_2 = 1

PLE_DIM = 256
RMS_EPS = 1e-6

RWKV_HEADS = 8
RWKV_HEAD_DIM = 64
RWKV_WIDTH = RWKV_HEADS * RWKV_HEAD_DIM
DECAY_LORA = 64
AAA_LORA = 64
GATE_LORA = 128
GN_EPS = 64e-5
RWKV_COLS = 3 * RWKV_WIDTH + DECAY_LORA + AAA_LORA + GATE_LORA

DIFF_HEADS = 4
DIFF_HEAD_DIM = 64
DIFF_QK_WIDTH = DIFF_HEADS * 2 * DIFF_HEAD_DIM
DIFF_V_DIM = 2 * DIFF_HEAD_DIM
DIFF_V_WIDTH = DIFF_HEADS * DIFF_V_DIM
DIFF_COLS = 2 * DIFF_QK_WIDTH + DIFF_V_WIDTH
ROPE_THETA = 10000.0
Q_BLOCK = 128

GATE_COLS = 2 * D_MODEL
IN_COLS = RWKV_COLS + DIFF_COLS + GATE_COLS

N_GROUPS = 4
EXPERTS_PER_GROUP = 8
N_EXPERTS = N_GROUPS * EXPERTS_PER_GROUP
TOP_K = 2
EXPERT_FF = 512
ROW_BLOCK = 128


def rms_norm(x, gain, eps=RMS_EPS):
    xf = x.astype(jnp.float32)
    y = xf * lax.rsqrt(jnp.mean(xf * xf, axis=-1, keepdims=True) + eps)
    return (y * gain.astype(jnp.float32)).astype(x.dtype)

def rope_tables(seq, dim):
    inv = ROPE_THETA ** (-jnp.arange(0, dim, 2, dtype=jnp.float32) / dim)
    ang = jnp.arange(seq, dtype=jnp.float32)[:, None] * inv[None, :]
    ang = jnp.concatenate([ang, ang], axis=-1)
    return jnp.cos(ang), jnp.sin(ang)

def apply_rope(x, cos, sin):
    c = cos[:, None, None, :]
    s = sin[:, None, None, :]
    x1, x2 = jnp.split(x, 2, axis=-1)
    rot = jnp.concatenate([-x2, x1], axis=-1)
    return (x.astype(jnp.float32) * c + rot.astype(jnp.float32) * s).astype(x.dtype)

def wkv7_scan(r, decay, k, kk, a, v):
    b, s, h, n = r.shape

    def step(state, inp):
        r_t, w_t, k_t, kk_t, a_t, v_t = inp
        sa = jnp.einsum('bhvk,bhk->bhv', state, -kk_t)
        state = (state * w_t[:, :, None, :]
                 + sa[..., None] * (kk_t * a_t)[:, :, None, :]
                 + v_t[..., None] * k_t[:, :, None, :])
        return state, jnp.einsum('bhvk,bhk->bhv', state, r_t)

    s0 = jnp.zeros((b, h, n, n), jnp.float32)
    xs = (jnp.swapaxes(r, 0, 1), jnp.swapaxes(decay, 0, 1), jnp.swapaxes(k, 0, 1),
          jnp.swapaxes(kk, 0, 1), jnp.swapaxes(a, 0, 1), jnp.swapaxes(v, 0, 1))
    _, y = lax.scan(step, s0, xs)
    return jnp.swapaxes(y, 0, 1)

def rwkv7_branch(pr, mu, w0, w2, a0, a2, g2, k_k, k_a, r_k, ln_w, ln_b):
    b, s, _ = pr.shape
    f32 = jnp.float32
    prev = jnp.pad(pr[:, :-1], ((0, 0), (1, 0), (0, 0)))
    xs = pr + (prev - pr) * mu
    c0 = RWKV_WIDTH
    r, k, v, xw, xa, xg = jnp.split(
        xs, [c0, 2 * c0, 3 * c0, 3 * c0 + DECAY_LORA, 3 * c0 + DECAY_LORA + AAA_LORA], axis=-1)
    w_log = -jax.nn.softplus(-(w0 + jnp.tanh(xw) @ w2).astype(f32)) - 0.5
    decay = jnp.exp(-jnp.exp(w_log))
    a = jax.nn.sigmoid((a0 + xa @ a2).astype(f32))
    g = jax.nn.sigmoid(xg) @ g2

    def heads(t):
        return t.reshape(b, s, RWKV_HEADS, RWKV_HEAD_DIM).astype(f32)

    kk = heads(k * k_k)
    kk = kk / jnp.maximum(jnp.sqrt(jnp.sum(kk * kk, axis=-1, keepdims=True)), 1e-12)
    k_mod = k.astype(f32) * (1.0 + (a - 1.0) * k_a.astype(f32))
    r_h, k_h, v_h = heads(r), heads(k_mod), heads(v)
    y = wkv7_scan(r_h, heads(decay), k_h, kk, heads(a), v_h)
    mean = jnp.mean(y, axis=-1, keepdims=True)
    var = jnp.mean(jnp.square(y - mean), axis=-1, keepdims=True)
    y = ((y - mean) * lax.rsqrt(var + GN_EPS)).reshape(b, s, RWKV_WIDTH)
    y = y * ln_w.astype(f32) + ln_b.astype(f32)
    bonus = jnp.sum(r_h * k_h * r_k.astype(f32), axis=-1, keepdims=True) * v_h
    out = (y + bonus.reshape(b, s, RWKV_WIDTH)) * g.astype(f32)
    return out.astype(pr.dtype)

def diff_attention_branch(pd, q_gain, k_gain, lq1, lk1, lq2, lk2, subln_w, lam_init, cos, sin):
    b, s, _ = pd.shape
    f32 = jnp.float32
    q, k, v = jnp.split(pd, [DIFF_QK_WIDTH, 2 * DIFF_QK_WIDTH], axis=-1)
    q = apply_rope(rms_norm(q.reshape(b, s, DIFF_HEADS, 2, DIFF_HEAD_DIM), q_gain), cos, sin)
    k = apply_rope(rms_norm(k.reshape(b, s, DIFF_HEADS, 2, DIFF_HEAD_DIM), k_gain), cos, sin)
    q = q.transpose(0, 2, 3, 1, 4)
    k = k.transpose(0, 2, 3, 1, 4)
    v = v.reshape(b, s, DIFF_HEADS, DIFF_V_DIM).transpose(0, 2, 1, 3)
    lam = (jnp.exp(jnp.sum(lq1.astype(f32) * lk1.astype(f32)))
           - jnp.exp(jnp.sum(lq2.astype(f32) * lk2.astype(f32))) + lam_init)
    scale = DIFF_HEAD_DIM ** -0.5
    neg = jnp.finfo(f32).min
    blocks = []
    for i in range(s // Q_BLOCK):
        q0 = i * Q_BLOCK
        end = q0 + Q_BLOCK
        sc = jnp.einsum('bhcqd,bhckd->bhcqk', q[:, :, :, q0:end], k[:, :, :, :end]).astype(f32) * scale
        causal = jnp.arange(end)[None, :] <= (q0 + jnp.arange(Q_BLOCK))[:, None]
        prob = jax.nn.softmax(jnp.where(causal, sc, neg), axis=-1)
        attn = prob[:, :, 0] - lam * prob[:, :, 1]
        blocks.append(jnp.einsum('bhqk,bhkv->bhqv', attn.astype(v.dtype), v[:, :, :end]))
    o = jnp.concatenate(blocks, axis=2)
    o = rms_norm(o, subln_w) * (1.0 - lam_init)
    return o.transpose(0, 2, 1, 3).reshape(b, s, DIFF_V_WIDTH)

def hierarchical_moe(h, w_group, b_group, w_er, b_er, w_gate, w_up, w_down):
    b, s, d = h.shape
    t = b * s
    f32 = jnp.float32
    hf = h.reshape(t, d)
    g_prob = jax.nn.softmax((hf @ w_group).astype(f32) + b_group.astype(f32), axis=-1)
    g_top, g_idx = lax.top_k(g_prob, 1)
    e_logits = ((hf @ w_er).astype(f32) + b_er.astype(f32)).reshape(t, N_GROUPS, EXPERTS_PER_GROUP)
    sel = jnp.broadcast_to(g_idx[:, :, None], (t, 1, EXPERTS_PER_GROUP))
    e_logits = jnp.take_along_axis(e_logits, sel, axis=1)[:, 0]
    e_top, e_idx = lax.top_k(e_logits, TOP_K)
    weights = g_top * jax.nn.softmax(e_top, axis=-1)
    expert_id = g_idx * EXPERTS_PER_GROUP + e_idx

    n_assign = t * TOP_K
    eid = expert_id.reshape(n_assign).astype(jnp.int32)
    tid = jnp.repeat(jnp.arange(t, dtype=jnp.int32), TOP_K)
    wt = weights.reshape(n_assign)
    order = jnp.argsort(eid)
    se = eid[order]
    counts = jnp.bincount(eid, length=N_EXPERTS).astype(jnp.int32)
    starts = jnp.cumsum(counts) - counts
    pcounts = ((counts + ROW_BLOCK - 1) // ROW_BLOCK) * ROW_BLOCK
    pends = jnp.cumsum(pcounts)
    pstarts = pends - pcounts
    dest = pstarts[se] + (jnp.arange(n_assign, dtype=jnp.int32) - starts[se])
    rows = n_assign + N_EXPERTS * ROW_BLOCK
    n_blocks = rows // ROW_BLOCK
    buf_tok = jnp.full((rows,), t, jnp.int32).at[dest].set(tid[order])
    buf_w = jnp.zeros((rows,), wt.dtype).at[dest].set(wt[order])
    blk_e = jnp.minimum(jnp.searchsorted(pends, jnp.arange(n_blocks, dtype=jnp.int32) * ROW_BLOCK,
                                         side='right'), N_EXPERTS - 1)
    hpad = jnp.concatenate([hf, jnp.zeros((1, d), hf.dtype)], axis=0)
    xs = hpad[buf_tok].reshape(n_blocks, ROW_BLOCK, d)

    def expert_block(args):
        xb, e = args
        return (jax.nn.silu(xb @ w_gate[e]) * (xb @ w_up[e])) @ w_down[e]

    yb = lax.map(expert_block, (xs, blk_e)).reshape(rows, d)
    yb = yb * buf_w[:, None].astype(yb.dtype)
    out = jax.ops.segment_sum(yb, buf_tok, num_segments=t + 1)[:t]
    return out.reshape(b, s, d)

def second_inputs(seed: int = 0) -> dict:
    key = jax.random.key(seed)
    ks = iter(jax.random.split(key, 40))
    L = DEPTH_2
    f32 = jnp.float32

    def nrm(shape, scale):
        return scale * jax.random.normal(next(ks), shape, f32)

    def gain(shape, base=1.0):
        return base + 0.1 * jax.random.normal(next(ks), shape, f32)

    return {
        'x': nrm((BATCH, SEQ, D_MODEL), 1.0),
        'p': nrm((L, BATCH, SEQ, PLE_DIM), 1.0),
        'norm_mix': gain((L, D_MODEL)),
        'w_in': nrm((L, D_MODEL, IN_COLS), D_MODEL ** -0.5),
        'rwkv_mu': jax.random.uniform(next(ks), (L, RWKV_COLS), f32),
        'rwkv_w0': jax.random.uniform(next(ks), (L, RWKV_WIDTH), f32, -6.0, 0.0),
        'rwkv_w2': nrm((L, DECAY_LORA, RWKV_WIDTH), DECAY_LORA ** -0.5),
        'rwkv_a0': nrm((L, RWKV_WIDTH), 0.5),
        'rwkv_a2': nrm((L, AAA_LORA, RWKV_WIDTH), AAA_LORA ** -0.5),
        'rwkv_g2': nrm((L, GATE_LORA, RWKV_WIDTH), GATE_LORA ** -0.5),
        'rwkv_k_k': gain((L, RWKV_WIDTH), 0.85),
        'rwkv_k_a': gain((L, RWKV_WIDTH)),
        'rwkv_r_k': gain((L, RWKV_HEADS, RWKV_HEAD_DIM), 0.5),
        'rwkv_ln_w': gain((L, RWKV_WIDTH)),
        'rwkv_ln_b': nrm((L, RWKV_WIDTH), 0.02),
        'q_norm': gain((L, DIFF_HEAD_DIM)),
        'k_norm': gain((L, DIFF_HEAD_DIM)),
        'lambda_q1': nrm((L, DIFF_HEAD_DIM), 0.1),
        'lambda_k1': nrm((L, DIFF_HEAD_DIM), 0.1),
        'lambda_q2': nrm((L, DIFF_HEAD_DIM), 0.1),
        'lambda_k2': nrm((L, DIFF_HEAD_DIM), 0.1),
        'subln_w': gain((L, DIFF_V_DIM)),
        'w_branch_rwkv': nrm((L, RWKV_WIDTH, D_MODEL), RWKV_WIDTH ** -0.5),
        'w_branch_diff': nrm((L, DIFF_V_WIDTH, D_MODEL), DIFF_V_WIDTH ** -0.5),
        'w_out': nrm((L, D_MODEL, D_MODEL), D_MODEL ** -0.5),
        'norm_ffn': gain((L, D_MODEL)),
        'w_group': nrm((L, D_MODEL, N_GROUPS), D_MODEL ** -0.5),
        'b_group': nrm((L, N_GROUPS), 0.01),
        'w_expert_router': nrm((L, D_MODEL, N_EXPERTS), D_MODEL ** -0.5),
        'b_expert_router': nrm((L, N_EXPERTS), 0.01),
        'w_gate': nrm((L, N_EXPERTS, D_MODEL, EXPERT_FF), D_MODEL ** -0.5),
        'w_up': nrm((L, N_EXPERTS, D_MODEL, EXPERT_FF), D_MODEL ** -0.5),
        'w_down': nrm((L, N_EXPERTS, EXPERT_FF, D_MODEL), EXPERT_FF ** -0.5),
        'norm_ple': gain((L, D_MODEL)),
        'w_ple_gate': nrm((L, D_MODEL, D_MODEL), D_MODEL ** -0.5),
        'w_ple_proj': nrm((L, PLE_DIM, D_MODEL), PLE_DIM ** -0.5),
    }

def second_block(x, p, norm_mix, w_in, rwkv_mu, rwkv_w0, rwkv_w2, rwkv_a0, rwkv_a2, rwkv_g2,
              rwkv_k_k, rwkv_k_a, rwkv_r_k, rwkv_ln_w, rwkv_ln_b, q_norm, k_norm,
              lambda_q1, lambda_k1, lambda_q2, lambda_k2, subln_w, w_branch_rwkv,
              w_branch_diff, w_out, norm_ffn, w_group, b_group, w_expert_router,
              b_expert_router, w_gate, w_up, w_down, norm_ple, w_ple_gate, w_ple_proj):
    seq = x.shape[1]
    cos, sin = rope_tables(seq, DIFF_HEAD_DIM)
    for l in range(DEPTH_2):
        lam_init = 0.8 - 0.6 * math.exp(-0.3 * l)
        h = rms_norm(x, norm_mix[l])
        proj = h @ w_in[l]
        p_rwkv = proj[..., :RWKV_COLS]
        p_diff = proj[..., RWKV_COLS:RWKV_COLS + DIFF_COLS]
        g_rwkv, g_diff = jnp.split(proj[..., RWKV_COLS + DIFF_COLS:], 2, axis=-1)
        o_rwkv = rwkv7_branch(p_rwkv, rwkv_mu[l], rwkv_w0[l], rwkv_w2[l], rwkv_a0[l], rwkv_a2[l],
                              rwkv_g2[l], rwkv_k_k[l], rwkv_k_a[l], rwkv_r_k[l], rwkv_ln_w[l],
                              rwkv_ln_b[l])
        o_diff = diff_attention_branch(p_diff, q_norm[l], k_norm[l], lambda_q1[l], lambda_k1[l],
                                       lambda_q2[l], lambda_k2[l], subln_w[l], lam_init, cos, sin)
        mixed = (jax.nn.sigmoid(g_rwkv) * (o_rwkv @ w_branch_rwkv[l])
                 + jax.nn.sigmoid(g_diff) * (o_diff @ w_branch_diff[l]))
        x = x + mixed @ w_out[l]
        x = x + hierarchical_moe(rms_norm(x, norm_ffn[l]), w_group[l], b_group[l],
                                 w_expert_router[l], b_expert_router[l], w_gate[l], w_up[l],
                                 w_down[l])
        ple_gate = jax.nn.sigmoid(rms_norm(x, norm_ple[l]) @ w_ple_gate[l])
        x = x + ple_gate * (p[l] @ w_ple_proj[l])
    return x


def setup_inputs(seed=0):
    out = dict(first_inputs(seed))
    for name, value in second_inputs(seed + 1).items():
        if name != "x":
            out[name + "_2"] = value
    return out


def reference(
    x, mem, ln_mix, ln_xattn, ln_mem, ln_ffn, final_norm, m_in_w, m_conv_w, m_conv_b, m_dt_bias,
    m_a_log, m_d, m_norm_w, m_out_w, h_in_w, h_lower_bounds, h_norm_w, h_out_w, g_in_w,
    g_conv_w, g_a_log, g_dt_bias, g_norm_w, g_out_w, xa_q, xa_kv, xa_o, f_up, f_conv_w,
    f_conv_b, f_down, p_2, norm_mix_2, w_in_2, rwkv_mu_2, rwkv_w0_2, rwkv_w2_2, rwkv_a0_2,
    rwkv_a2_2, rwkv_g2_2, rwkv_k_k_2, rwkv_k_a_2, rwkv_r_k_2, rwkv_ln_w_2, rwkv_ln_b_2,
    q_norm_2, k_norm_2, lambda_q1_2, lambda_k1_2, lambda_q2_2, lambda_k2_2, subln_w_2,
    w_branch_rwkv_2, w_branch_diff_2, w_out_2, norm_ffn_2, w_group_2, b_group_2,
    w_expert_router_2, b_expert_router_2, w_gate_2, w_up_2, w_down_2, norm_ple_2, w_ple_gate_2,
    w_ple_proj_2,
):
    x = first_block(
        x, mem, ln_mix, ln_xattn, ln_mem, ln_ffn, final_norm, m_in_w, m_conv_w, m_conv_b,
        m_dt_bias, m_a_log, m_d, m_norm_w, m_out_w, h_in_w, h_lower_bounds, h_norm_w, h_out_w,
        g_in_w, g_conv_w, g_a_log, g_dt_bias, g_norm_w, g_out_w, xa_q, xa_kv, xa_o, f_up,
        f_conv_w, f_conv_b, f_down,
    )
    return second_block(
        x, p_2, norm_mix_2, w_in_2, rwkv_mu_2, rwkv_w0_2, rwkv_w2_2, rwkv_a0_2, rwkv_a2_2,
        rwkv_g2_2, rwkv_k_k_2, rwkv_k_a_2, rwkv_r_k_2, rwkv_ln_w_2, rwkv_ln_b_2, q_norm_2,
        k_norm_2, lambda_q1_2, lambda_k1_2, lambda_q2_2, lambda_k2_2, subln_w_2,
        w_branch_rwkv_2, w_branch_diff_2, w_out_2, norm_ffn_2, w_group_2, b_group_2,
        w_expert_router_2, b_expert_router_2, w_gate_2, w_up_2, w_down_2, norm_ple_2,
        w_ple_gate_2, w_ple_proj_2,
    )


_drawn_inputs = setup_inputs


def setup_inputs(seed=0):
    import zlib

    import numpy as np

    out = dict(_drawn_inputs(seed))
    spreads = {}
    factors = {'ln_xattn': 3.755,
     'ln_mem': 3.092,
     'h_lower_bounds': 6.684,
     'f_conv_b': 3.03,
     'rwkv_ln_b_2': 4.698,
     'lambda_k2_2': 3.491,
     'b_group_2': 4.239,
     'b_expert_router_2': 12.938,
     'norm_ple_2': 3.701}
    for name, (base, spread) in spreads.items():
        noise = np.random.default_rng([zlib.crc32(name.encode()), seed]).standard_normal(out[name].shape)
        drawn = base * np.exp(spread * noise) if base else spread * noise
        out[name] = __import__('jax').numpy.asarray(drawn.astype(out[name].dtype))
    for name, factor in factors.items():
        out[name] = (out[name] * factor).astype(out[name].dtype)
    return out
```

```python
from contextlib import ExitStack, contextmanager

import concourse.bass as bass
from concourse import mybir
import numpy as np

F32, F32R = mybir.dt.float32, mybir.dt.float32r
ALU = mybir.AluOpType
ACT = mybir.ActivationFunctionType
AX = mybir.AxisListType

P = 128
SEQ = 256
D = 1024
TT = SEQ // P
KB = D // P
EPS = 1e-6
RING = 6
PAGE = 2048
D_FF = 2816
FFN_CHUNKS = D_FF // 256
EXPERTS = 32
EXPERT_FF = 512
BIG = 1.0e30

PLAN = ["mamba0", "xattn0", "ffn0", "hgrn1", "xattn1", "ffn1", "gdn2", "xattn2", "ffn2",
        "mamba3", "xattn3", "ffn3", "final0", "mixtwo0", "moe0", "ple0"]


def split_stage(stage):
    return stage[:-1], int(stage[-1])


def constant_tables():
    i = np.arange(P)
    col, row = i[:, None], i[None, :]
    upto = (col <= row).astype(np.float32)
    t = {
        "ident": np.eye(P),
        "ones": np.ones((P, P)),
        "upto3": np.concatenate([upto, np.ones((P, P)), upto], 1),
        "before": (col < row),
        "after": (col > row),
        "since": (col >= row),
        "blk64": (col // 64 == row // 64),
        "gla": (col // 32 == row // 32) & (col <= row),
        "half2": np.stack([i < 64, i >= 64], 1),
    }
    lev = [((row // b) % 2 == 1) & (col // b == row // b - 1) for b in (1, 2, 4, 8, 16, 32, 64)]
    t["join_t"] = np.concatenate(lev, 1)
    t["join1"] = lev[0].T
    tok = np.arange(SEQ)
    t["restart32"] = np.broadcast_to(tok % 32 != 0, (P, SEQ))
    t["restart128"] = np.broadcast_to(tok % 128 != 0, (P, SEQ))
    inv = (np.float32(10000.0) ** (-np.arange(0, 64, 2, dtype=np.float32) / np.float32(64))).astype(np.float32)
    ang = tok.astype(np.float32)[:, None] * inv[None, :]
    ang = np.concatenate([ang, ang], 1)
    sign = np.where(np.arange(64) < 32, -1.0, 1.0)
    t["cos"] = np.cos(ang).reshape(TT, P, 64).transpose(1, 0, 2).reshape(P, -1)
    t["sin"] = (np.sin(ang) * sign).reshape(TT, P, 64).transpose(1, 0, 2).reshape(P, -1)
    t["rank4"] = np.broadcast_to(4.0 - np.arange(4), (P, 4))
    t["rank32"] = np.broadcast_to(32.0 - np.arange(32), (P, 32))
    allowed = np.where(col >= row, 0.0, -BIG)
    t["causal3"] = np.concatenate([allowed, np.zeros((P, P)), allowed], 1)
    t["eps"] = np.broadcast_to([EPS, 64e-5], (P, 2))
    at, parts, n = {}, [], 0
    for name, a in t.items():
        a = np.ascontiguousarray(a, dtype=np.float32)
        at[name] = (n, a.shape[1])
        parts.append(a)
        n += a.shape[1]
    return np.concatenate(parts, 1), at


COLS = [("ln_mix", 4 * 8), ("ln_xattn", 4 * 8), ("ln_mem", 4 * 8), ("ln_ffn", 4 * 8),
        ("m_conv_w", 2 * 4 * 32), ("m_conv_b", 2 * 32), ("m_norm_w", 2 * 16),
        ("h_lower_bounds", 4 * 8), ("h_norm_w", 1),
        ("g_conv_w", 4 * 32), ("g_norm_w", 1),
        ("f_conv_w", 4 * 3 * 22), ("f_conv_b", 4 * 22),
        ("norm_mix_2", 8), ("rwkv_mu_2", 14), ("rwkv_w0_2", 4), ("rwkv_a0_2", 4), ("rwkv_k_k_2", 4),
        ("rwkv_k_a_2", 4), ("rwkv_r_k_2", 4), ("subln_w_2", 1), ("norm_ffn_2", 8), ("norm_ple_2", 8)]
ROWS = [("m_dt_bias", 64), ("m_a_log", 64), ("m_d", 64), ("g_a_log", 16), ("g_dt_bias", 16),
        ("q_norm_2", 64), ("k_norm_2", 64), ("lambda_q1_2", 64), ("lambda_k1_2", 64), ("lambda_q2_2", 64),
        ("lambda_k2_2", 64), ("b_group_2", 4), ("b_expert_router_2", 32),
        ("rwkv_ln_w_2", 512), ("rwkv_ln_b_2", 512)]
SMALLS = [("m_dt_w", 2 * 8 * 32), ("g_ba_w", 8 * 32), ("router_w", 8 * 36), ("lora_w", 512), ("gate_w", 512)]


def offsets(table):
    at, n = {}, 0
    for name, w in table:
        at[name] = n
        n += w
    return at, n


COL_AT, N_COLS = offsets(COLS)
ROW_AT, N_ROWS = offsets(ROWS)
SMALL_AT, N_SMALL = offsets(SMALLS)
CONSTS, CONST_AT = constant_tables()


def pages_of(stage):
    kind = split_stage(stage)[0]
    return {"mamba": 32, "hgrn": 20, "gdn": 32, "xattn": 16, "ffn": 33, "final": 0,
            "mixtwo": 21 + 2 + 2 + 4, "moe": 6 * EXPERTS, "ple": 5}[kind]


class Program:

    def __init__(self, eng, sems, name):
        self.eng, self.sems, self.name = eng, sems, name
        self.given, self.taken = {}, {}
        self.i, self.rates, self.page = None, {}, 0
        self.next_stage = None

    def value(self, count, sem):
        if self.i is None:
            return count
        assert sem in self.rates, (self.name, sem)
        return self.i * self.rates[sem] + count

    def take(self, sem, n=1):
        self.taken[sem] = self.taken.get(sem, 0) + n
        return self.value(self.taken[sem], sem)

    def ahead(self, sem, n):
        return self.value(self.taken[sem] + n, sem)

    def one(self, sem):
        self.given[sem] = self.given.get(sem, 0) + 1
        return 1

    def own(self, sem):
        return self.value(self.given[sem], sem)

    marks = {}

    def mark(self, name, sem):
        self.marks[name] = (sem, self.given.get(sem, 0))

    def marked(self, name):
        return self.marks[name][0]

    def reach(self, name, n=0):
        return self.marks[name][1] + n

    @contextmanager
    def repeat(self, n, **rates):
        if n == 1:
            yield 0
            return
        before = (dict(self.given), dict(self.taken), self.page)
        with self.eng.Fori(0, n) as i:
            self.i, self.rates = i, rates
            yield i
            self.i = None
        for now, was in ((self.given, before[0]), (self.taken, before[1])):
            for sem in now:
                step = now[sem] - was.get(sem, 0)
                if step:
                    assert step == rates[sem], (self.name, sem, step, rates)
                    now[sem] = was.get(sem, 0) + n * step
        self.page = before[2] + n * (self.page - before[2])


class Semaphores(dict):
    def __init__(self, nc, ctx):
        super().__init__()
        self.nc, self.ctx = nc, ctx

    def __missing__(self, name):
        self[name] = self.ctx.enter_context(self.nc.semaphore(name))
        return self[name]


def build(nc, x_in, mem_in, p_in, pages_in, consts_in, cols_in, rows_in, smalls_in, final_in, out):
    total_pages = sum(pages_of(s) for s in PLAN)
    with ExitStack() as ctx:
        def sb(name, *shape):
            return ctx.enter_context(nc.sbuf_tensor(name, [P, *shape], F32))

        def two_views(name, *shape):
            with nc.sbuf_tensor(name, [P, *shape], F32) as plain:
                pass
            return plain, ctx.enter_context(nc.sbuf_tensor(name + "_r", [P, *shape], F32R))

        sems = Semaphores(nc, ctx)
        ps = ctx.enter_context(nc.psum_tensor("ps", [P, 8, 512], F32))
        ring, ring_r = two_views("ring", RING, PAGE)
        x = sb("x", TT, D)
        hT, hT_r = two_views("hT", KB, SEQ)
        memT = sb("memT", KB, SEQ)
        bufA, bufA_r = two_views("bufA", 32 * (SEQ + 3))
        bufB, bufB_r = two_views("bufB", 4096)
        bufC, bufC_r = two_views("bufC", 4096)
        bufE, bufE_r = two_views("bufE", 4096)
        yT, yT_r = two_views("yT", 16, SEQ)
        consts = sb("consts", CONSTS.shape[1])
        cols = sb("cols", N_COLS)
        rows = sb("rows", N_ROWS)
        smalls = sb("smalls", N_SMALL)
        st = sb("st", 1024)
        xn = bufE[:, 0:TT * D].rearrange("p (t d) -> p t d", t=TT)

        def const(name, lo=0, n=None):
            a, w = CONST_AT[name]
            return consts[:, a + lo:a + (w if n is None else lo + n)]

        def col(name, j):
            return cols[:, bass.ds(COL_AT[name] + j, 1)]

        def row(name, lo=0, n=None):
            w = dict(ROWS)[name] if n is None else n
            return rows[:, ROW_AT[name] + lo:ROW_AT[name] + lo + w]

        def small(name):
            return smalls[:, SMALL_AT[name]:SMALL_AT[name] + dict(SMALLS)[name]]

        ident = const("ident")
        ones = const("ones")

        def bank(b, lo=0, n=512):
            return ps[:, b, lo:lo + n]


        def norm_act(e, src):
            e.eng.wait_ge(sems["x_ready"], e.take("x_ready"))
            sum_roots_act(e, src)

        def sum_roots_act(e, src):
            for t in range(TT):
                ins = nc.scalar.activation(xn[:, t, :], src[:, t, :], ACT.Square, accum_out=st[:, t:t + 1])
            ins.then_inc(sems["scalar_step"], e.one("scalar_step"))
            e.eng.wait_ge(sems["scalar_step"], e.own("scalar_step"))
            nc.scalar.activation(st[:, 2:2 + TT], st[:, 0:TT], ACT.Sqrt, bias=const("eps", 0, 1), scale=1.0 / D) \
                .then_inc(sems["roots_ready"], e.one("roots_ready"))

        def norm_dve(e, src):
            e.eng.wait_ge(sems["roots_ready"], e.take("roots_ready"))
            nc.vector.reciprocal(st[:, 4:4 + TT], st[:, 2:2 + TT]).then_inc(sems["vector_step"], e.one("vector_step"))
            e.eng.wait_ge(sems["vector_step"], e.own("vector_step"))
            for t in range(TT):
                nc.vector.tensor_scalar(xn[:, t, :], src[:, t, :], st[:, 4 + t:5 + t], None, ALU.mult) \
                    .then_inc(sems["normed_ready"], e.one("normed_ready"))

        def norm_pe(e):
            e.eng.wait_ge(sems["normed_ready"], e.take("normed_ready", 2))
            turn_pe(e, lambda kb, t: xn[:, t, kb * P:(kb + 1) * P], KB // 2)

        def turn_pe(e, src, groups):
            for g in range(groups):
                if g >= 2:
                    done = ("turned_out_act", "turned_out_dve")[g % 2]
                    e.eng.wait_ge(sems[done], e.take(done))
                for j in range(2):
                    for t in range(TT):
                        ins = nc.tensor.transpose(bank(2 + g % 2, (2 * j + t) * P, P), src(2 * g + j, t), ident)
                done = ("turned_act", "turned_dve")[g % 2]
                ins.then_inc(sems[done], e.one(done))
            e.eng.wait_ge(sems["turned_out_act"], e.take("turned_out_act"))
            if groups > 1:
                e.eng.wait_ge(sems["turned_out_dve"], e.take("turned_out_dve"))

        def turn_act(e, dst, groups, gain=None):
            for g in range(0, groups, 2):
                e.eng.wait_ge(sems["turned_act"], e.take("turned_act"))
                for j in range(2):
                    scale = 1.0 if gain is None else gain(2 * g + j)
                    ins = nc.scalar.activation(dst(2 * g + j), bank(2, j * 256, 256), ACT.Copy, scale=scale)
                ins.then_inc(sems["turned_out_act"], e.one("turned_out_act"))

        def turn_dve(e, dst, groups, gain=None):
            for g in range(1, groups, 2):
                e.eng.wait_ge(sems["turned_dve"], e.take("turned_dve"))
                for j in range(2):
                    scale = 1.0 if gain is None else gain(2 * g + j)
                    ins = nc.vector.tensor_scalar(dst(2 * g + j), bank(3, j * 256, 256), scale, None, ALU.mult)
                ins.then_inc(sems["turned_out_dve"], e.one("turned_out_dve"))

        def page_in(e):
            slot = e.page % RING
            count = 16 * (e.page // RING + 1)
            e.eng.wait_ge(sems[f"page_landed_{slot}"], count if e.i is None else e.i * 16 + count)
            e.page += 1
            return slot

        def page_products(e, n=1):
            e.page += n
            e.eng.wait_ge(sems["page_done"], e.value(e.page, "page_done"))

        def page_wide_fm(e, hsrc, b):
            slot = page_in(e)
            for m in range(2):
                for kb in range(KB):
                    ins = nc.tensor.matmul(bank(b, m * 256, 256), ring[:, slot, kb * 256 + m * P:kb * 256 + (m + 1) * P],
                                           hsrc[:, kb, :], start=kb == 0, stop=kb == KB - 1)
            ins.then_inc(sems["page_done"], e.one("page_done"))

        def page_wide_tm(e, hsrc, b):
            slot = page_in(e)
            for t in range(TT):
                for kb in range(KB):
                    ins = nc.tensor.matmul(bank(b, t * 256, 256), hsrc[:, kb, t * P:(t + 1) * P],
                                           ring[:, slot, kb * 256:(kb + 1) * 256], start=kb == 0, stop=kb == KB - 1)
            ins.then_inc(sems["page_done"], e.one("page_done"))

        def page_deep(e, act, first, last, b=4):
            slot = page_in(e)
            for k in range(2):
                for t in range(TT):
                    for half in range(2):
                        ins = nc.tensor.matmul(bank(b + 2 * t + half), act(k)[:, t * P:(t + 1) * P],
                                               ring[:, slot, k * D + half * 512:k * D + (half + 1) * 512],
                                               start=first and k == 0, stop=last and k == 1)
            ins.then_inc(sems["page_done"], e.one("page_done"))

        def project_pe(e, n, page_fn, hsrc, phase=0):
            def some(k):
                for j in range(k):
                    e.eng.wait_ge(sems["projected_out"], e.take("projected_out"))
                    page_fn(e, hsrc, (j + phase) % 2)
            whole = n // RING if n >= 2 * RING else 0
            if whole:
                with e.repeat(whole, projected_out=RING, page_done=RING):
                    some(RING)
            some(n - whole * RING)

        def project_act(e, n, copy, **rates):
            whole = n // 2 if n >= 8 else 0
            if whole:
                with e.repeat(whole, projected_out=2, page_done=2, **rates) as i:
                    for j in range(2):
                        page_products(e)
                        copy(e, i * 2 + j, j).then_inc(sems["projected_out"], e.one("projected_out"))
            for j in range(2 * whole, n):
                page_products(e)
                copy(e, j, j % 2).then_inc(sems["projected_out"], e.one("projected_out"))

        def down_pe(e, n, act):
            for j in range(n):
                page_deep(e, lambda k: act(2 * j + k), j == 0, j == n - 1)

        def residual_dve(e, n):
            if e.next_stage is not None and split_stage(e.next_stage)[0] == "xattn":
                e.page += n
                xattn_open_dve(e, split_stage(e.next_stage)[1])
                e.page -= n
            page_products(e, n)
            for t in range(TT):
                for half in range(2):
                    part = x[:, t, half * 512:(half + 1) * 512]
                    ins = nc.vector.tensor_tensor(part, part, bank(4 + 2 * t + half), ALU.add)
            ins.then_inc(sems["x_ready"], e.one("x_ready"))

        mem = bufA[:, 0:TT * D].rearrange("p (t d) -> p t d", t=TT)

        def memory_act(e):
            e.eng.wait_ge(sems["memory_loaded"], 16)
            sum_roots_act(e, mem)
            turn_act(e, lambda kb: memT[:, kb, :], KB // 2)

        def memory_dve(e):
            e.eng.wait_ge(sems["memory_loaded"], 16)
            norm_dve(e, mem)
            turn_dve(e, lambda kb: memT[:, kb, :], KB // 2)
            e.eng.wait_ge(sems["turned_out_dve"], e.own("turned_out_dve"))

        def normed_act(e, gain):
            norm_act(e, x)
            turn_act(e, lambda kb: hT[:, kb, :], KB // 2, gain)

        def normed_dve(e, gain):
            norm_dve(e, x)
            turn_dve(e, lambda kb: hT[:, kb, :], KB // 2, gain)

        glu_highs = [yT_r[:, 0:8, :].rearrange("p k s -> p (k s)"), yT_r[:, 8:16, :].rearrange("p k s -> p (k s)"),
                     bufE_r[:, 2048:4096]]
        xattn_highs = [bufA_r[:, j * PAGE:(j + 1) * PAGE] for j in range(1, 4)]
        HIGHS = 3

        def page_low(slot):
            return ring_r[:, slot, :]

        def split_page_act(e, n, highs=glu_highs):
            page = e.page + n
            slot, count = page % RING, 16 * (page // RING + 1)
            e.eng.wait_ge(sems[f"page_landed_{slot}"], count if e.i is None else e.i * 16 + count)
            if page >= HIGHS:
                e.eng.wait_ge(sems["page_done"], e.value(page - HIGHS + 1, "page_done"))
            nc.scalar.copy(highs[page % HIGHS], ring[:, slot, :]) \
                .then_inc(sems["page_high_ready"], e.one("page_high_ready"))

        def split_page_dve(e, n, highs=glu_highs):
            page = e.page + n
            slot = page % RING
            e.eng.wait_ge(sems["page_high_ready"], e.take("page_high_ready"))
            nc.vector.tensor_tensor(page_low(slot), ring[:, slot, :], highs[page % HIGHS], ALU.subtract) \
                .then_inc(sems["page_split"], e.one("page_split"))

        def split_page_pe(e, highs):
            slot, high = e.page % RING, highs[e.page % HIGHS]
            e.page += 1
            e.eng.wait_ge(sems["page_split"], e.take("page_split"))
            return high, page_low(slot)

        def split_wide_pe(e, b, t_high, t_low, highs=glu_highs):
            high, low = split_page_pe(e, highs)
            for m in range(2):
                for kb in range(KB):
                    at = slice(kb * 256 + m * P, kb * 256 + (m + 1) * P)
                    out_ = bank(b, m * 256, 256)
                    nc.tensor.matmul(out_, high[:, at], t_high[:, kb, :], start=kb == 0, stop=False)
                    nc.tensor.matmul(out_, high[:, at], t_low[:, kb, :], start=False, stop=False)
                    ins = nc.tensor.matmul(out_, low[:, at], t_high[:, kb, :], start=False, stop=kb == KB - 1)
            ins.then_inc(sems["page_done"], e.one("page_done"))

        def split_wide_tm_pe(e, b, t_high, t_low, highs):
            high, low = split_page_pe(e, highs)
            for t in range(TT):
                for kb in range(KB):
                    at, tok = slice(kb * 256, (kb + 1) * 256), slice(t * P, (t + 1) * P)
                    out_ = bank(b, t * 256, 256)
                    nc.tensor.matmul(out_, t_high[:, kb, tok], high[:, at], start=kb == 0, stop=False)
                    nc.tensor.matmul(out_, t_high[:, kb, tok], low[:, at], start=False, stop=False)
                    ins = nc.tensor.matmul(out_, t_low[:, kb, tok], high[:, at], start=False, stop=kb == KB - 1)
            ins.then_inc(sems["page_done"], e.one("page_done"))

        def split_deep_pe(e, a_high, a_low, first, last, highs=glu_highs):
            high, low = split_page_pe(e, highs)
            for k in range(2):
                for t in range(TT):
                    tok = slice(t * P, (t + 1) * P)
                    for half in range(2):
                        at = slice(k * D + half * 512, k * D + (half + 1) * 512)
                        out_ = bank(4 + 2 * t + half)
                        nc.tensor.matmul(out_, a_high[:, k, tok], high[:, at], start=first and k == 0, stop=False)
                        nc.tensor.matmul(out_, a_high[:, k, tok], low[:, at], start=False, stop=False)
                        ins = nc.tensor.matmul(out_, a_low[:, k, tok], high[:, at], start=False, stop=last and k == 1)
            ins.then_inc(sems["page_done"], e.one("page_done"))

        def split_turn_pe(e):
            e.eng.wait_ge(sems["normed_ready"], e.take("normed_ready", 2))
            for g in range(KB // 2):
                if g >= 2:
                    e.eng.wait_ge(sems["turned_split"], e.take("turned_split"))
                for j in range(2):
                    for t in range(TT):
                        kb = 2 * g + j
                        ins = nc.tensor.transpose(bank(2 + g % 2, (2 * j + t) * P, P),
                                                  xn[:, t, kb * P:(kb + 1) * P], ident)
                ins.then_inc(sems["turned"], e.one("turned"))
            e.eng.wait_ge(sems["turned_split"], e.take("turned_split", 2))

        def split_turn_act(e, high, gain):
            for g in range(KB // 2):
                e.eng.wait_ge(sems["turned"], e.take("turned"))
                for j in range(2):
                    kb = 2 * g + j
                    ins = nc.scalar.activation(high[:, kb, :], bank(2 + g % 2, j * 256, 256), ACT.Copy, scale=gain(kb))
                ins.then_inc(sems["turned_high"], e.one("turned_high"))

        def split_turn_dve(e, high, low, gain):
            for g in range(KB // 2):
                e.eng.wait_ge(sems["turned_high"], e.take("turned_high"))
                for j in range(2):
                    kb = 2 * g + j
                    ins = nc.vector.scalar_tensor_tensor(low[:, kb, :], bank(2 + g % 2, j * 256, 256), gain(kb),
                                                         high[:, kb, :], ALU.mult, ALU.subtract)
                ins.then_inc(sems["turned_split"], e.one("turned_split"))

        XH = 4
        kT = bufB[:, 0:2048].rearrange("p (k m) -> p k m", k=KB)
        xv = bufB[:, 2048:4096].rearrange("p (m d) -> p m d", m=TT)
        memG_high = bufE_r[:, 2048:4096].rearrange("p (k m) -> p k m", k=KB)
        memG_low = bufC_r[:, 0:2048].rearrange("p (k m) -> p k m", k=KB)
        q_high, q_low = yT_r[:, 8:16, :], hT_r[:, :, :]
        y_high, y_low = yT_r[:, 8:16, :], yT_r[:, 0:8, :]
        qT = bufC[:, 2048:4096].rearrange("p (k s) -> p k s", k=KB)
        probs = bufE[:, 2048:4096].rearrange("p (h t m) -> p h t m", h=XH, t=TT)
        probsT = bufA[:, 0:2048].rearrange("p (h m s) -> p h m s", h=XH, m=TT)

        def xattn_pe(e, l):
            e.eng.wait_ge(sems["parts_split"], e.take("parts_split"))
            for j in range(12):
                if j == 8:
                    split_turn_pe(e)
                e.eng.wait_ge(sems["projected_out"], e.take("projected_out"))
                if j < 4:
                    split_wide_pe(e, j % 2, memG_high, memG_low, xattn_highs)
                elif j < 8:
                    split_wide_tm_pe(e, j % 2, memG_high, memG_low, xattn_highs)
                else:
                    split_wide_pe(e, j % 2, q_high, q_low, xattn_highs)
            e.eng.wait_ge(sems["projected_out"], e.ahead("projected_out", 2))
            for h in range(XH):
                for t in range(TT):
                    for k in range(2):
                        ins = nc.tensor.matmul(bank(4 + h, t * 256, 256), qT[:, 2 * h + k, t * P:(t + 1) * P],
                                               kT[:, 2 * h + k, :], start=k == 0, stop=k == 1)
                ins.then_inc(sems["scores_ready"], e.one("scores_ready"))
            for h in range(XH):
                e.eng.wait_ge(sems["probs_ready"], e.take("probs_ready"))
                if h >= 2:
                    done = ("turned_out_act", "turned_out_dve")[h % 2]
                    e.eng.wait_ge(sems[done], e.take(done))
                for m in range(TT):
                    for t in range(TT):
                        ins = nc.tensor.transpose(bank(2 + h % 2, (2 * m + t) * P, P),
                                                  probs[:, h, t, m * P:(m + 1) * P], ident)
                done = ("turned_act", "turned_dve")[h % 2]
                ins.then_inc(sems[done], e.one(done))
            for h in range(XH):
                if h >= 2:
                    done = ("turned_out_act", "turned_out_dve")[h % 2]
                    e.eng.wait_ge(sems[done], e.take(done))
                    e.eng.wait_ge(sems["head_out_done"], e.take("head_out_done"))
                for dh in range(2):
                    for m in range(TT):
                        ins = nc.tensor.matmul(bank(h % 2, dh * 256, 256),
                                               xv[:, m, h * 256 + dh * P:h * 256 + (dh + 1) * P],
                                               probsT[:, h, m, :], start=m == 0, stop=m == 1)
                ins.then_inc(sems["head_ready"], e.one("head_ready"))
            e.eng.wait_ge(sems["head_out_done"], e.take("head_out_done", 2))
            for j in range(4):
                split_deep_pe(e, y_high[:, 2 * j:2 * j + 2, :], y_low[:, 2 * j:2 * j + 2, :], j == 0, j == 3, xattn_highs)

        def xattn_act(e, l):
            split_page_act(e, 0, xattn_highs)
            if e.page < HIGHS:
                e.eng.wait_ge(sems["x_ready"], 1)
            for kb in range(KB):
                ins = nc.scalar.activation(memG_high[:, kb, :], memT[:, kb, :], ACT.Copy, scale=col("ln_mem", l * KB + kb))
            ins.then_inc(sems["high_ready"], e.one("high_ready"))
            split_page_act(e, 1, xattn_highs)
            split_page_act(e, 2, xattn_highs)
            norm_act(e, x)
            for j in range(12):
                page_products(e)
                into = kT[:, 2 * j:2 * j + 2, :] if j < 4 else xv[:, :, (j - 4) * 256:(j - 3) * 256] if j < 8 else \
                    qT[:, 2 * j - 16:2 * j - 14, :]
                nc.scalar.copy(into, bank(j % 2)).then_inc(sems["projected_out"], e.one("projected_out"))
                if j == 7:
                    split_turn_act(e, q_high, lambda kb: col("ln_xattn", l * KB + kb))
                if j < 11:
                    split_page_act(e, 2, xattn_highs)
            for h in range(XH):
                e.eng.wait_ge(sems["score_max_ready"], e.take("score_max_ready"))
                for t in range(TT):
                    ins = nc.scalar.activation(probs[:, h, t, :], bank(4 + h, t * 256, 256), ACT.Exp,
                                               bias=st[:, 8 + 2 * h + t:9 + 2 * h + t], scale=1.0 / 16.0,
                                               accum_out=st[:, 16 + 2 * h + t:17 + 2 * h + t])
                ins.then_inc(sems["exp_ready"], e.one("exp_ready"))
            split_page_act(e, 2, xattn_highs)
            for h in (0, 2):
                e.eng.wait_ge(sems["turned_act"], e.take("turned_act"))
                nc.scalar.copy(probsT[:, h, :, :], bank(2)).then_inc(sems["turned_out_act"], e.one("turned_out_act"))
            for h in range(XH):
                e.eng.wait_ge(sems["head_ready"], e.take("head_ready"))
                nc.scalar.copy(y_high[:, 2 * h:2 * h + 2, :], bank(h % 2)) \
                    .then_inc(sems["high_ready"], e.one("high_ready"))
            split_page_act(e, 3, xattn_highs)
            e.page += 4

        def xattn_open_dve(e, l):
            split_page_dve(e, 0, xattn_highs)
            e.eng.wait_ge(sems["high_ready"], e.take("high_ready"))
            for kb in range(KB):
                ins = nc.vector.scalar_tensor_tensor(memG_low[:, kb, :], memT[:, kb, :], col("ln_mem", l * KB + kb),
                                                     memG_high[:, kb, :], ALU.mult, ALU.subtract)
            ins.then_inc(sems["parts_split"], e.one("parts_split"))
            split_page_dve(e, 1, xattn_highs)

        def xattn_dve(e, l):
            split_page_dve(e, 2, xattn_highs)
            norm_dve(e, x)
            for j in range(3, 10):
                split_page_dve(e, j, xattn_highs)
            split_turn_dve(e, q_high, q_low, lambda kb: col("ln_xattn", l * KB + kb))
            for j in range(10, 14):
                split_page_dve(e, j, xattn_highs)
            e.page += 12
            for h in range(XH):
                e.eng.wait_ge(sems["scores_ready"], e.take("scores_ready"))
                nc.vector.tensor_reduce(st[:, 8 + 2 * h:10 + 2 * h],
                                        bank(4 + h).rearrange("p (t m) -> p t m", t=TT), AX.X, ALU.max) \
                   .then_inc(sems["vector_step"], e.one("vector_step"))
                e.eng.wait_ge(sems["vector_step"], e.own("vector_step"))
                nc.vector.tensor_scalar(st[:, 8 + 2 * h:10 + 2 * h], st[:, 8 + 2 * h:10 + 2 * h],
                                        -1.0 / 16.0, None, ALU.mult) \
                    .then_inc(sems["score_max_ready"], e.one("score_max_ready"))
            for h in range(XH):
                e.eng.wait_ge(sems["exp_ready"], e.take("exp_ready"))
                nc.vector.reciprocal(st[:, 24 + 2 * h:26 + 2 * h], st[:, 16 + 2 * h:18 + 2 * h]) \
                   .then_inc(sems["vector_step"], e.one("vector_step"))
                e.eng.wait_ge(sems["vector_step"], e.own("vector_step"))
                for t in range(TT):
                    ins = nc.vector.tensor_scalar(probs[:, h, t, :], probs[:, h, t, :],
                                                  st[:, 24 + 2 * h + t:25 + 2 * h + t], None, ALU.mult)
                ins.then_inc(sems["probs_ready"], e.one("probs_ready"))
            split_page_dve(e, 2, xattn_highs)
            for h in (1, 3):
                e.eng.wait_ge(sems["turned_dve"], e.take("turned_dve"))
                nc.vector.tensor_copy(probsT[:, h, :, :], bank(3)) \
                    .then_inc(sems["turned_out_dve"], e.one("turned_out_dve"))
            for h in range(XH):
                e.eng.wait_ge(sems["high_ready"], e.take("high_ready"))
                nc.vector.tensor_tensor(y_low[:, 2 * h:2 * h + 2, :], bank(h % 2).rearrange("p (k s) -> p k s", k=2),
                                        y_high[:, 2 * h:2 * h + 2, :], ALU.subtract) \
                    .then_inc(sems["head_out_done"], e.one("head_out_done"))
            split_page_dve(e, 3, xattn_highs)
            residual_dve(e, 4)

        gpad = bufB[:, 0:4 * (SEQ + 2)].rearrange("p (c m s) -> p c m s", c=2, m=2)
        conv = bufB[:, 1040:1040 + 1024].rearrange("p (c m s) -> p c m s", c=2, m=2)
        hid = bufE[:, 1024:1024 + 512].rearrange("p (m s) -> p m s", m=2)
        hid_high = bufB_r[:, 2080:2080 + 1024].rearrange("p (c m s) -> p c m s", c=2, m=2)
        hid_low = bufE_r[:, 0:1024].rearrange("p (c m s) -> p c m s", c=2, m=2)
        hT_high = bufC_r[:, 0:2048].rearrange("p (k s) -> p k s", k=KB)
        hT_low = bufC_r[:, 2048:4096].rearrange("p (k s) -> p k s", k=KB)
        expert_w = bufA[:, 0:EXPERTS * SEQ].rearrange("p (e s) -> p e s", e=EXPERTS)

        def split_tokens_act(e):
            e.eng.wait_ge(sems["turned_out_act"], e.own("turned_out_act"))
            for kb in (0, 4):
                ins = nc.scalar.copy(hT_high[:, kb:kb + 2, :], hT[:, kb:kb + 2, :])
            ins.then_inc(sems["high_ready"], e.one("high_ready"))

        def split_tokens_dve(e):
            e.eng.wait_ge(sems["turned_out_dve"], e.own("turned_out_dve"))
            for kb in (2, 6):
                ins = nc.vector.tensor_copy(hT_high[:, kb:kb + 2, :], hT[:, kb:kb + 2, :])
            ins.then_inc(sems["vector_step"], e.one("vector_step"))
            e.eng.wait_ge(sems["vector_step"], e.own("vector_step"))
            e.eng.wait_ge(sems["high_ready"], e.take("high_ready"))
            nc.vector.tensor_tensor(hT_low, hT[:, :, :], hT_high, ALU.subtract) \
                .then_inc(sems["parts_split"], e.one("parts_split"))

        def glu_pe(e, chunks):
            def up(odd):
                split_wide_pe(e, 2 * odd, hT_high, hT_low)
                split_wide_pe(e, 2 * odd + 1, hT_high, hT_low)

            def body(odd, first=False, last=False):
                if not last:
                    up(1 - odd)
                e.eng.wait_ge(sems["hidden_ready"], e.take("hidden_ready"))
                split_deep_pe(e, hid_high[:, odd, :, :], hid_low[:, odd, :, :], first, last)

            up(0)
            body(0, first=True)
            pairs = (chunks - 2) // 2
            with e.repeat(pairs, hidden_ready=2, page_split=6, page_done=6):
                body(1)
                body(0)
            for c in range(1 + 2 * pairs, chunks):
                body(c % 2, last=c == chunks - 1)

        def glu_chunks(e, chunks, body, **rates):
            body(0, 0, 0, first=True)
            pairs = (chunks - 2) // 2
            with e.repeat(pairs, page_done=6, **rates) as i:
                body(i * 2 + 1, i, 1)
                body(i * 2 + 2, i + 1, 0)
            for c in range(1 + 2 * pairs, chunks):
                body(c, c // 2, c % 2, last=c == chunks - 1)

        def after_page(e, n):
            e.eng.wait_ge(sems["page_done"], e.value(e.page + n, "page_done"))

        def ffn_act(e, l):
            norm_act(e, x)
            split_page_act(e, 0)
            split_turn_act(e, hT_high, lambda kb: col("ln_ffn", l * KB + kb))
            split_page_act(e, 1)
            e.eng.wait_ge(sems["pad_cleared"], e.take("pad_cleared"))

            def body(c, half, odd, first=False, last=False):
                after_page(e, 1)
                nc.scalar.copy(gpad[:, odd, :, 2:], bank(2 * odd)).then_inc(sems["gate_ready"], e.one("gate_ready"))
                e.page += 2 if first else 3
                if not last:
                    split_page_act(e, 0)
                e.eng.wait_ge(sems["conv_ready"], e.take("conv_ready"))
                nc.scalar.activation(conv[:, odd, :, :], conv[:, odd, :, :], ACT.Silu) \
                    .then_inc(sems["silu_ready"], e.one("silu_ready"))
                if last:
                    split_page_act(e, 0)
                    e.page += 1
                else:
                    split_page_act(e, 1)
                    split_page_act(e, 2)
            glu_chunks(e, FFN_CHUNKS, body, gate_ready=2, conv_ready=2, silu_ready=2, page_high_ready=6)

        def hidden_dve(e, odd, weight=None, used="silu_used"):
            e.eng.wait_ge(sems["silu_ready"], e.take("silu_ready"))
            after_page(e, 2)
            nc.vector.tensor_tensor(hid, conv[:, odd, :, :], bank(2 * odd + 1).rearrange("p (m s) -> p m s", m=2),
                                    ALU.mult).then_inc(sems[used], e.one(used))
            e.eng.wait_ge(sems[used], e.own(used))
            if weight is not None:
                nc.vector.tensor_tensor(hid, hid, weight, ALU.mult) \
                    .then_inc(sems["vector_step"], e.one("vector_step"))
                e.eng.wait_ge(sems["vector_step"], e.own("vector_step"))
            nc.vector.tensor_copy(hid_high[:, odd, :, :], hid) \
                .then_inc(sems["vector_step"], e.one("vector_step"))
            e.eng.wait_ge(sems["vector_step"], e.own("vector_step"))
            nc.vector.tensor_tensor(hid_low[:, odd, :, :], hid, hid_high[:, odd, :, :], ALU.subtract) \
                .then_inc(sems["hidden_ready"], e.one("hidden_ready"))

        def glu_pages_dve(e, odd, first, last, hidden):
            if not last:
                n = 2 if first else 3
                split_page_dve(e, n)
                hidden()
                e.page += n
                split_page_dve(e, 1)
                split_page_dve(e, 2)
                e.eng.wait_ge(sems["hidden_ready"], e.own("hidden_ready"))
            else:
                hidden()
                e.page += 3
                split_page_dve(e, 0)
                e.page += 1

        def ffn_dve(e, l):
            nc.vector.memset(gpad[:, :, :, 0:2], 0.0).then_inc(sems["pad_cleared"], e.one("pad_cleared"))
            norm_dve(e, x)
            split_page_dve(e, 0)
            split_turn_dve(e, hT_high, hT_low, lambda kb: col("ln_ffn", l * KB + kb))
            split_page_dve(e, 1)

            def body(c, half, odd, first=False, last=False):
                e.eng.wait_ge(sems["gate_ready"], e.take("gate_ready"))
                for tap in (2, 1, 0):
                    for m in range(2):
                        w = col("f_conv_w", (l * 3 + tap) * 22 + c * 2 + m)
                        src, dst = gpad[:, odd, m, tap:tap + SEQ], conv[:, odd, m, :]
                        if tap == 2:
                            ins = nc.vector.tensor_scalar(dst, src, w, col("f_conv_b", l * 22 + c * 2 + m),
                                                          ALU.mult, ALU.add)
                        else:
                            ins = nc.vector.scalar_tensor_tensor(dst, src, w, dst, ALU.mult, ALU.add)
                    if tap:
                        ins.then_inc(sems["vector_step"], e.one("vector_step"))
                        e.eng.wait_ge(sems["vector_step"], e.own("vector_step"))
                ins.then_inc(sems["conv_ready"], e.one("conv_ready"))
                glu_pages_dve(e, odd, first, last, lambda: hidden_dve(e, odd))
            glu_chunks(e, FFN_CHUNKS, body, gate_ready=2, vector_step=6, conv_ready=2, silu_ready=2, silu_used=2,
                       hidden_ready=2, page_high_ready=6, page_split=6)
            residual_dve(e, 0)

        def ffn_pe(e, l):
            split_turn_pe(e)
            glu_pe(e, FFN_CHUNKS)

        final_gain = bufB[:, 0:D]

        def final_act(e):
            norm_act(e, x)
            e.eng.dma_start(final_gain, final_in.to_broadcast([P, D])).then_inc(sems["final_gain_loaded"], 16)

        def final_dve(e):
            e.eng.wait_ge(sems["roots_ready"], e.take("roots_ready"))
            nc.vector.reciprocal(st[:, 4:4 + TT], st[:, 2:2 + TT]).then_inc(sems["vector_step"], e.one("vector_step"))
            e.eng.wait_ge(sems["vector_step"], e.own("vector_step"))
            e.eng.wait_ge(sems["final_gain_loaded"], 16)
            for t in range(TT):
                ins = nc.vector.scalar_tensor_tensor(x[:, t, :], x[:, t, :], st[:, 4 + t:5 + t], final_gain,
                                                     ALU.mult, ALU.mult)
            ins.then_inc(sems["x_ready"], e.one("x_ready"))

        def moe_pe(e):
            norm_pe(e)
            w = small("router_w").rearrange("p (k n) -> p k n", k=KB)
            for t in range(TT):
                for kb in range(KB):
                    ins = nc.tensor.matmul(bank(0, 64 * t, 36), hT[:, kb, t * P:(t + 1) * P], w[:, kb, :],
                                           start=kb == 0, stop=kb == KB - 1)
            ins.then_inc(sems["narrow_ready"], e.one("narrow_ready"))
            e.eng.wait_ge(sems["token_weights_ready"], e.take("token_weights_ready"))
            for t in range(TT):
                ins = nc.tensor.transpose(bank(1, t * P, P)[0:EXPERTS, :], token_w[:, t, :], ident)
            ins.then_inc(sems["weights_turned"], e.one("weights_turned"))
            e.eng.wait_ge(sems["weights_out"], e.take("weights_out"))
            for k in range(EXPERTS // 2):
                if k >= 2:
                    e.eng.wait_ge(sems["weights_spread_out"], e.take("weights_spread_out"))
                for j in range(2):
                    ins = nc.tensor.matmul(bank(2 + k % 2, j * 256, 256),
                                           ident[0:EXPERTS, 2 * k + j:2 * k + j + 1].to_broadcast([EXPERTS, P]),
                                           weightsT[0:EXPERTS, :], start=True, stop=True)
                ins.then_inc(sems["weights_spread"], e.one("weights_spread"))
            e.eng.wait_ge(sems["weights_spread_out"], e.take("weights_spread_out", 2))
            e.eng.wait_ge(sems["parts_split"], e.take("parts_split"))
            glu_pe(e, 2 * EXPERTS)

        token_w = bufC[:, 0:64].rearrange("p (t n) -> p t n", t=TT)
        weightsT = bufC[:, 64:64 + SEQ]
        rt = bufC[:, 512:2048]

        def moe_act(e):
            normed_act(e, lambda kb: col("norm_ffn_2", kb))
            e.eng.wait_ge(sems["exponent_ready"], e.take("exponent_ready"))
            nc.scalar.activation(st[:, 64:64 + 10], st[:, 48:48 + 10], ACT.Exp) \
                .then_inc(sems["exponential_ready"], e.one("exponential_ready"))
            for k in range(EXPERTS // 2):
                e.eng.wait_ge(sems["weights_spread"], e.take("weights_spread"))
                nc.scalar.copy(expert_w[:, 2 * k:2 * k + 2, :], bank(2 + k % 2)) \
                    .then_inc(sems["weights_spread_out"], e.one("weights_spread_out"))

            split_page_act(e, 0)
            split_page_act(e, 1)
            split_tokens_act(e)

            def body(c, half, odd, first=False, last=False):
                after_page(e, 1)
                e.eng.wait_ge(sems["expert_silu_used"], e.take("expert_silu_used"))
                nc.scalar.activation(conv[:, odd, :, :], bank(2 * odd), ACT.Silu) \
                    .then_inc(sems["silu_ready"], e.one("silu_ready"))
                e.page += 2 if first else 3
                split_page_act(e, 0)
                if last:
                    e.page += 1
                else:
                    split_page_act(e, 1)
                    split_page_act(e, 2)
            glu_chunks(e, 2 * EXPERTS, body, silu_ready=2, expert_silu_used=2, page_high_ready=6)

        def moe_dve(e):
            normed_dve(e, lambda kb: col("norm_ffn_2", kb))
            e.eng.wait_ge(sems["narrow_ready"], e.take("narrow_ready"))
            lg = rt[:, 0:128].rearrange("p (t n) -> p t n", t=TT)
            gl, el = lg[:, :, 0:4], lg[:, :, 4:36]
            for t in range(TT):
                nc.vector.tensor_tensor(lg[:, t, 0:4], bank(0, 64 * t, 4), row("b_group_2"), ALU.add)
                ins = nc.vector.tensor_tensor(lg[:, t, 4:36], bank(0, 64 * t + 4, 32), row("b_expert_router_2"), ALU.add)
            ins.then_inc(sems["vector_step"], e.one("vector_step"))
            e.eng.wait_ge(sems["vector_step"], e.own("vector_step"))

            def wide(ap, n):
                return ap.unsqueeze(2).to_broadcast([P, TT, n])

            def first_max(v, n, mx, hot, rank):
                r3 = rank.unsqueeze(1).to_broadcast([P, TT, n])
                nc.vector.tensor_reduce(mx, v, AX.X, ALU.max).then_inc(sems["vector_step"], e.one("vector_step"))
                e.eng.wait_ge(sems["vector_step"], e.own("vector_step"))
                nc.vector.tensor_tensor(hot, v, wide(mx, n), ALU.is_equal) \
                   .then_inc(sems["vector_step"], e.one("vector_step"))
                e.eng.wait_ge(sems["vector_step"], e.own("vector_step"))
                nc.vector.tensor_tensor(hot, hot, r3, ALU.mult).then_inc(sems["vector_step"], e.one("vector_step"))
                e.eng.wait_ge(sems["vector_step"], e.own("vector_step"))
                nc.vector.tensor_reduce(st[:, 44:46], hot, AX.X, ALU.max) \
                   .then_inc(sems["vector_step"], e.one("vector_step"))
                e.eng.wait_ge(sems["vector_step"], e.own("vector_step"))
                nc.vector.tensor_tensor(hot, r3, wide(st[:, 44:46], n), ALU.is_equal) \
                   .then_inc(sems["vector_step"], e.one("vector_step"))
                e.eng.wait_ge(sems["vector_step"], e.own("vector_step"))

            hot4 = rt[:, 128:136].rearrange("p (t n) -> p t n", t=TT)
            hot_a = rt[:, 160:224].rearrange("p (t n) -> p t n", t=TT)
            hot_b = rt[:, 224:288].rearrange("p (t n) -> p t n", t=TT)
            inside = rt[:, 288:352].rearrange("p (t n) -> p t n", t=TT)
            first_max(gl, 4, st[:, 36:38], hot4, const("rank4"))
            nc.vector.tensor_tensor(st[:, 48:56].rearrange("p (t n) -> p t n", t=TT), gl, wide(st[:, 36:38], 4),
                                    ALU.subtract).then_inc(sems["vector_step"], e.one("vector_step"))
            e.eng.wait_ge(sems["vector_step"], e.own("vector_step"))
            for t in range(TT):
                ins = nc.vector.tensor_copy(inside[:, t, :].rearrange("p (g k) -> p g k", g=4),
                                            hot4[:, t, :].unsqueeze(2).to_broadcast([P, 4, 8]))
            ins.then_inc(sems["vector_step"], e.one("vector_step"))
            e.eng.wait_ge(sems["vector_step"], e.own("vector_step"))
            nc.vector.tensor_tensor(el, el, inside, ALU.mult).then_inc(sems["vector_step"], e.one("vector_step"))
            e.eng.wait_ge(sems["vector_step"], e.own("vector_step"))
            nc.vector.tensor_scalar(inside, inside, 1.0, BIG, ALU.subtract, ALU.mult) \
               .then_inc(sems["vector_step"], e.one("vector_step"))
            e.eng.wait_ge(sems["vector_step"], e.own("vector_step"))
            nc.vector.tensor_tensor(el, el, inside, ALU.add).then_inc(sems["vector_step"], e.one("vector_step"))
            e.eng.wait_ge(sems["vector_step"], e.own("vector_step"))
            first_max(el, 32, st[:, 38:40], hot_a, const("rank32"))
            nc.vector.scalar_tensor_tensor(el, hot_a, -BIG, el, ALU.mult, ALU.add) \
               .then_inc(sems["vector_step"], e.one("vector_step"))
            e.eng.wait_ge(sems["vector_step"], e.own("vector_step"))
            first_max(el, 32, st[:, 40:42], hot_b, const("rank32"))
            nc.vector.tensor_tensor(st[:, 56:58], st[:, 40:42], st[:, 38:40], ALU.subtract) \
                .then_inc(sems["exponent_ready"], e.one("exponent_ready"))
            e.eng.wait_ge(sems["exponential_ready"], e.take("exponential_ready"))
            nc.vector.tensor_reduce(st[:, 80:82], st[:, 64:72].rearrange("p (t n) -> p t n", t=TT), AX.X, ALU.add) \
               .then_inc(sems["vector_step"], e.one("vector_step"))
            e.eng.wait_ge(sems["vector_step"], e.own("vector_step"))
            nc.vector.tensor_scalar(st[:, 82:84], st[:, 72:74], 1.0, None, ALU.add) \
               .then_inc(sems["vector_step"], e.one("vector_step"))
            e.eng.wait_ge(sems["vector_step"], e.own("vector_step"))
            nc.vector.tensor_tensor(st[:, 80:82], st[:, 80:82], st[:, 82:84], ALU.mult) \
               .then_inc(sems["vector_step"], e.one("vector_step"))
            e.eng.wait_ge(sems["vector_step"], e.own("vector_step"))
            nc.vector.reciprocal(st[:, 84:86], st[:, 80:82]).then_inc(sems["vector_step"], e.one("vector_step"))
            e.eng.wait_ge(sems["vector_step"], e.own("vector_step"))
            nc.vector.tensor_tensor(st[:, 86:88], st[:, 84:86], st[:, 72:74], ALU.mult) \
               .then_inc(sems["vector_step"], e.one("vector_step"))
            e.eng.wait_ge(sems["vector_step"], e.own("vector_step"))
            nc.vector.tensor_tensor(hot_a, hot_a, wide(st[:, 84:86], 32), ALU.mult) \
               .then_inc(sems["vector_step"], e.one("vector_step"))
            e.eng.wait_ge(sems["vector_step"], e.own("vector_step"))
            nc.vector.tensor_tensor(hot_b, hot_b, wide(st[:, 86:88], 32), ALU.mult) \
               .then_inc(sems["vector_step"], e.one("vector_step"))
            e.eng.wait_ge(sems["vector_step"], e.own("vector_step"))
            nc.vector.tensor_tensor(token_w, hot_a, hot_b, ALU.add) \
                .then_inc(sems["token_weights_ready"], e.one("token_weights_ready"))
            e.eng.wait_ge(sems["weights_turned"], e.take("weights_turned"))
            nc.vector.tensor_copy(weightsT[0:EXPERTS, :], bank(1, 0, 256)[0:EXPERTS, :]) \
                .then_inc(sems["weights_out"], e.one("weights_out"))
            for odd in range(2):
                nc.vector.memset(st[:, 113 + odd:114 + odd], 0.0).then_inc(sems["expert_silu_used"], e.one("expert_silu_used"))
            split_page_dve(e, 0)
            split_page_dve(e, 1)
            e.eng.wait_ge(sems["weights_spread_out"], e.take("weights_spread_out", EXPERTS // 2))
            split_tokens_dve(e)

            def body(c, expert, odd, first=False, last=False):
                glu_pages_dve(e, odd, first, last, lambda: hidden_dve(
                    e, odd, expert_w[:, bass.ds(expert, 1), :].to_broadcast([P, 2, SEQ]), "expert_silu_used"))
            glu_chunks(e, 2 * EXPERTS, body, silu_ready=2, expert_silu_used=2, vector_step=4, hidden_ready=2,
                       page_high_ready=6, page_split=6)
            residual_dve(e, 0)

        ple_in = bufB[:, 0:512].rearrange("p (t d) -> p t d", t=TT)
        pleT = bufB[:, 512:1024].rearrange("p (k s) -> p k s", k=2)
        sig = bufC[:, 0:2048].rearrange("p (b n) -> p b n", b=4)

        def ple_pe(e):
            norm_pe(e)
            e.eng.wait_ge(sems["ple_loaded"], 16)
            for k in range(2):
                for t in range(TT):
                    ins = nc.tensor.transpose(bank(2, (2 * k + t) * P, P), ple_in[:, t, k * P:(k + 1) * P], ident)
            ins.then_inc(sems["turned_act"], e.one("turned_act"))
            e.eng.wait_ge(sems["turned_out_act"], e.take("turned_out_act"))
            page_deep(e, lambda k: pleT[:, k, :], True, True, b=0)
            down_pe(e, 4, lambda kb: hT[:, kb, :])

        def ple_act(e):
            norm_act(e, x)
            e.eng.dma_start(ple_in, p_in).then_inc(sems["ple_loaded"], 16)
            turn_act(e, lambda kb: hT[:, kb, :], KB // 2, lambda kb: col("norm_ple_2", kb))
            e.eng.wait_ge(sems["turned_act"], e.take("turned_act"))
            nc.scalar.copy(pleT[:, :, :], bank(2)).then_inc(sems["turned_out_act"], e.one("turned_out_act"))
            page_products(e, 5)
            for b in range(4):
                ins = nc.scalar.activation(sig[:, b, :], bank(4 + b), ACT.Sigmoid)
            ins.then_inc(sems["ple_gate_ready"], e.one("ple_gate_ready"))

        def ple_dve(e):
            normed_dve(e, lambda kb: col("norm_ple_2", kb))
            e.page += 5
            e.eng.wait_ge(sems["ple_gate_ready"], e.take("ple_gate_ready"))
            for b in range(4):
                ins = nc.vector.tensor_tensor(sig[:, b, :], sig[:, b, :], bank(b), ALU.mult)
            ins.then_inc(sems["vector_step"], e.one("vector_step"))
            e.eng.wait_ge(sems["vector_step"], e.own("vector_step"))
            for t in range(TT):
                for half in range(2):
                    part = x[:, t, half * 512:(half + 1) * 512]
                    ins = nc.vector.tensor_tensor(part, part, sig[:, 2 * t + half, :], ALU.add)
            ins.then_inc(sems["x_ready"], e.one("x_ready"))

        CW = 4
        PADW = SEQ + CW - 1
        conved = bufA[:, 0:32 * PADW].rearrange("p (c s) -> p c s", c=32)
        acc = bufE[:, 2048:3072].rearrange("p (o m s) -> p o m s", o=2, m=2)

        def conv_project_act(e, pages):
            def one(p, odd):
                tiles = bass.ds(2 * p, 2)
                page_products(e)
                nc.scalar.copy(conved[:, tiles, CW - 1:], bank(odd)).then_inc(sems["raw_ready"], e.one("raw_ready"))
                e.eng.wait_ge(sems["taps_ready"], e.take("taps_ready"))
                e.eng.nop(nofuse=True)
                nc.scalar.activation(conved[:, tiles, CW - 1:], acc[:, odd, :, :], ACT.Silu) \
                    .then_inc(sems["projected_out"], e.one("projected_out"))
            with e.repeat(pages // 2, page_done=2, raw_ready=2, taps_ready=2, projected_out=2) as i:
                for odd in range(2):
                    one(i * 2 + odd, odd)

        def conv_project_dve(e, pages, weight, bias):
            nc.vector.memset(conved[:, :, 0:CW - 1], 0.0) \
                .then_inc(sems["vector_step"], e.one("vector_step"))
            e.eng.wait_ge(sems["vector_step"], e.own("vector_step"))
            with e.repeat(pages // 2, raw_ready=2, taps_ready=2, vector_step=2 * (CW - 1)) as i:
                for odd in range(2):
                    e.eng.wait_ge(sems["raw_ready"], e.take("raw_ready"))
                    for tap in range(CW - 1, -1, -1):
                        for m in range(2):
                            tile = i * 4 + 2 * odd + m
                            src, dst = conved[:, bass.ds(tile, 1), tap:tap + SEQ], acc[:, odd, m:m + 1, :]
                            if tap == CW - 1:
                                ins = nc.vector.tensor_scalar(dst, src, weight(tap, tile), bias(tile) if bias else 0.0,
                                                              ALU.mult, ALU.add)
                            else:
                                ins = nc.vector.scalar_tensor_tensor(dst, src, weight(tap, tile), dst, ALU.mult, ALU.add)
                        if tap:
                            ins.then_inc(sems["vector_step"], e.one("vector_step"))
                            e.eng.wait_ge(sems["vector_step"], e.own("vector_step"))
                    ins.then_inc(sems["taps_ready"], e.one("taps_ready"))

        def silu_columns(dst):
            def copy(e, j, b):
                e.eng.nop(nofuse=True)
                return nc.scalar.activation(dst[:, :, bass.ds(j * 256, 256)], bank(b), ACT.Silu)
            return copy

        def narrow_pe(e, w, b, n, done):
            w = w.rearrange("p (k n) -> p k n", k=KB)
            for t in range(TT):
                for kb in range(KB):
                    ins = nc.tensor.matmul(bank(b, 64 * t, n), hT[:, kb, t * P:(t + 1) * P], w[:, kb, :],
                                           start=kb == 0, stop=kb == KB - 1)
            ins.then_inc(sems[done], e.one(done))

        def s2(lo, n):
            return st[:, lo:lo + TT * n].rearrange("p (t n) -> p t n", t=TT)

        def softplus_act(e, ap):
            e.eng.wait_ge(sems["softplus_arg_ready"], e.take("softplus_arg_ready"))
            nc.scalar.activation(ap, ap, ACT.Exp).then_inc(sems["scalar_step"], e.one("scalar_step"))
            e.eng.wait_ge(sems["scalar_step"], e.own("scalar_step"))
            nc.scalar.activation(ap, ap, ACT.Ln, bias=const("ones", 0, 1)) \
                .then_inc(sems["softplus_log_ready"], e.one("softplus_log_ready"))

        def softplus_dve(e, v, ap):
            nc.vector.tensor_scalar(ap, v, -1.0, None, ALU.mult).then_inc(sems["vector_step"], e.one("vector_step"))
            e.eng.wait_ge(sems["vector_step"], e.own("vector_step"))
            nc.vector.tensor_tensor(ap, v, ap, ALU.min) \
                .then_inc(sems["softplus_arg_ready"], e.one("softplus_arg_ready"))
            e.eng.wait_ge(sems["softplus_log_ready"], e.take("softplus_log_ready"))
            nc.vector.scalar_tensor_tensor(v, v, 0.0, ap, ALU.max, ALU.add) \
               .then_inc(sems["vector_step"], e.one("vector_step"))
            e.eng.wait_ge(sems["vector_step"], e.own("vector_step"))

        yflat = yT[:, :, :].rearrange("p k s -> p (k s)")
        upto, upto3 = const("upto3", 0, P), const("upto3")

        MH, MG, MP = 32, 8, 64
        mz = bufB[:, :].rearrange("p (t n) -> p t n", t=TT)
        mx = bufC[:, :].rearrange("p (t n) -> p t n", t=TT)
        my = bufE[:, :].rearrange("p (t n) -> p t n", t=TT)
        cb = bufA[:, 0:MG * 384].rearrange("p (g n) -> p g n", g=MG)
        m_decay = yflat[:, 0:3 * 384].rearrange("p (o n) -> p o n", o=3)
        m_mix = yflat[:, 1152:2304].rearrange("p (o n) -> p o n", o=3)
        m_rows = yflat[:, 2304:2304 + SEQ]
        m_dt, m_dta, m_sum, m_log = s2(128, 32), s2(192, 32), s2(256, 32), s2(320, 32)
        m_a = st[:, 384:416]
        m_ss, m_root, m_rec = s2(416, MG), s2(432, MG), s2(448, MG)

        def mamba_pe(e, l):
            norm_pe(e)
            a = l // 3
            narrow_pe(e, small("m_dt_w")[:, a * 256:(a + 1) * 256], 4, MH, "narrow_ready")
            project_pe(e, 16, page_wide_fm, hT)
            project_pe(e, 8, page_wide_tm, hT)
            e.eng.wait_ge(sems["step_decays_ready"], e.take("step_decays_ready"))
            nc.tensor.matmul(bank(5, 0, MH), upto, m_dta[:, 0, :], start=True, stop=True)
            nc.tensor.matmul(bank(5, MH, MH), ones, m_dta[:, 0, :], start=True, stop=False)
            nc.tensor.matmul(bank(5, MH, MH), upto, m_dta[:, 1, :], start=False, stop=True)
            r = bank(5, 128, SEQ)[0:MH, :]
            nc.tensor.matmul(r[:, 0:P], m_dta[:, 0, :], upto, start=True, stop=True)
            nc.tensor.matmul(r[:, P:], m_dta[:, 0, :], ones, start=True, stop=False)
            nc.tensor.matmul(r[:, P:], m_dta[:, 1, :], upto, start=False, stop=True) \
                .then_inc(sems["sums_ready"], e.one("sums_ready"))
            e.eng.wait_ge(sems["projected_out"], e.ahead("projected_out", 2))
            turn_pe(e, lambda ct, t: conved[:, ct, CW - 1 + t * P:CW - 1 + (t + 1) * P], 8)
            for g in range(MG):
                if g >= 2:
                    e.eng.wait_ge(sems["cb_masked"], e.take("cb_masked"))
                bT, cT = conved[:, 16 + g, CW - 1:], conved[:, 24 + g, CW - 1:]
                nc.tensor.matmul(bank(g % 2, 0, 256), bT[:, 0:P], cT, start=True, stop=True)
                nc.tensor.matmul(bank(g % 2, 256, P), bT[:, P:], cT[:, P:], start=True, stop=True) \
                    .then_inc(sems["cb_ready"], e.one("cb_ready"))
            e.eng.wait_ge(sems["cb_masked"], e.take("cb_masked", 2))
            e.eng.wait_ge(sems["inputs_scaled"], e.take("inputs_scaled"))

            def spread(h):
                nc.tensor.matmul(bank(2 + h % 2, 0, SEQ), ident[0:MH, h:h + 1].to_broadcast([MH, P]),
                                 m_rows[0:MH, :], start=True, stop=True) \
                    .then_inc(sems["decay_row_ready"], e.one("decay_row_ready"))

            e.mark(f"heads_{l}", "head_done")
            spread(0)
            spread(1)
            for h in range(MH):
                e.eng.wait_ge(sems["decay_arg_ready"], e.take("decay_arg_ready"))
                if h + 2 < MH:
                    spread(h + 2)
                e.eng.wait_ge(sems["mix_ready"], e.take("mix_ready"))
                b, at = 4 + 2 * (h // 8 % 2), (h % 8) * MP
                if h % 8 == 0 and h >= 16:
                    e.eng.wait_ge(sems["heads_out"], e.take("heads_out"))
                x0, x1 = mx[:, 0, h * MP:(h + 1) * MP], mx[:, 1, h * MP:(h + 1) * MP]
                w, new = m_mix[:, h % 3, :], h % 8 == 0
                nc.tensor.matmul(bank(b, at, MP), w[:, 0:P], x0, start=new, stop=True, skip_group_check=True)
                nc.tensor.matmul(bank(b + 1, at, MP), w[:, P:256], x0, start=new, stop=False, skip_group_check=True)
                ins = nc.tensor.matmul(bank(b + 1, at, MP), w[:, 256:], x1, start=False, stop=True, skip_group_check=True)
                ins.then_inc(sems["head_done"], e.one("head_done"))
            e.eng.wait_ge(sems["heads_out"], e.take("heads_out", 2))
            e.eng.wait_ge(sems["gated_ready"], e.take("gated_ready", 2))
            turn_pe(e, lambda kb, t: my[:, t, kb * P:(kb + 1) * P], 8)
            down_pe(e, 8, lambda kb: yT[:, kb, :])

        def mamba_act(e, l):
            a = l // 3
            normed_act(e, lambda kb: col("ln_mix", l * KB + kb))
            nc.scalar.activation(m_a, row("m_a_log", a * MH, MH), ACT.Exp) \
                .then_inc(sems["rates_ready"], e.one("rates_ready"))
            softplus_act(e, m_log)
            conv_project_act(e, 16)
            project_act(e, 8, silu_columns(mz))
            turn_act(e, lambda ct: mx[:, :, ct * P:(ct + 1) * P], 8)
            e.mark(f"x_turned_{l}", "turned_out_act")

            def squares(k):
                e.eng.wait_ge(sems["square_sums_ready"], e.take("square_sums_ready"))
                for t in range(TT):
                    for g in (2 * k, 2 * k + 1):
                        at = MG * 384 + (t * MG + g) * 256
                        ins = nc.scalar.activation(bufA[:, at:at + 256], my[:, t, g * 256:(g + 1) * 256], ACT.Square,
                                                   accum_out=m_ss[:, t, g:g + 1])
                ins.then_inc(sems["scalar_step"], e.one("scalar_step"))
                e.eng.wait_ge(sems["scalar_step"], e.own("scalar_step"))
            for h in range(MH):
                e.eng.wait_ge(sems["decay_arg_ready"], e.take("decay_arg_ready"))
                nc.scalar.activation(m_decay[:, h % 3, :], m_decay[:, h % 3, :], ACT.Exp) \
                    .then_inc(sems["decay_ready"], e.one("decay_ready"))
                if h in (11, 19, 27):
                    squares(h // 8 - 1)
            squares(3)
            nc.scalar.activation(m_root, m_ss, ACT.Sqrt, bias=const("eps", 0, 1), scale=1.0 / 256) \
                .then_inc(sems["roots_ready"], e.one("roots_ready"))
            turn_act(e, lambda kb: yT[:, kb, :], 8, lambda kb: col("m_norm_w", a * 16 + kb))
            e.page += 8

        def group_norm_root_act(e, root, ss, n, eps=0):
            e.eng.wait_ge(sems["square_sums_ready"], e.take("square_sums_ready"))
            nc.scalar.activation(root, ss, ACT.Sqrt, bias=const("eps", eps, 1), scale=1.0 / n) \
                .then_inc(sems["roots_ready"], e.one("roots_ready"))

        def group_scale_dve(e, y, sq, ss, root, rec, n):
            for t in range(TT):
                ins = nc.vector.tensor_tensor(sq[:, t, :], y[:, t, :], y[:, t, :], ALU.mult)
            ins.then_inc(sems["vector_step"], e.one("vector_step"))
            e.eng.wait_ge(sems["vector_step"], e.own("vector_step"))
            for t in range(TT):
                ins = nc.vector.tensor_reduce(ss[:, t, :], sq[:, t, :].rearrange("p (g n) -> p g n", n=n), AX.X, ALU.add)
            ins.then_inc(sems["square_sums_ready"], e.one("square_sums_ready"))
            e.eng.wait_ge(sems["roots_ready"], e.take("roots_ready"))
            nc.vector.reciprocal(rec, root).then_inc(sems["vector_step"], e.one("vector_step"))
            e.eng.wait_ge(sems["vector_step"], e.own("vector_step"))
            g = y.shape[2] // n
            for t in range(TT):
                v = y[:, t, :].rearrange("p (g n) -> p g n", n=n)
                ins = nc.vector.tensor_tensor(v, v, rec[:, t, :].unsqueeze(2).to_broadcast([P, g, n]), ALU.mult)
            return ins

        def mamba_dve(e, l):
            a = l // 3
            normed_dve(e, lambda kb: col("ln_mix", l * KB + kb))
            e.eng.wait_ge(sems["narrow_ready"], e.take("narrow_ready"))
            for t in range(TT):
                ins = nc.vector.tensor_tensor(m_dt[:, t, :], bank(4, 64 * t, MH), row("m_dt_bias", a * MH, MH), ALU.add)
            ins.then_inc(sems["vector_step"], e.one("vector_step"))
            e.eng.wait_ge(sems["vector_step"], e.own("vector_step"))
            softplus_dve(e, m_dt, m_log)
            e.eng.wait_ge(sems["rates_ready"], e.take("rates_ready"))
            nc.vector.scalar_tensor_tensor(m_dta, m_dt, -1.0, m_a.unsqueeze(1).to_broadcast([P, TT, MH]),
                                           ALU.mult, ALU.mult) \
                .then_inc(sems["step_decays_ready"], e.one("step_decays_ready"))
            conv_project_dve(e, 16, lambda tap, c: col("m_conv_w", c + (a * CW + tap) * 32),
                             lambda c: col("m_conv_b", c + a * 32))
            e.page += 24
            e.eng.wait_ge(sems["sums_ready"], e.take("sums_ready"))
            nc.vector.tensor_copy(m_sum, bank(5, 0, 2 * MH).rearrange("p (t n) -> p t n", t=TT))
            nc.vector.tensor_copy(m_rows[0:MH, :], bank(5, 128, SEQ)[0:MH, :])
            turn_dve(e, lambda ct: mx[:, :, ct * P:(ct + 1) * P], 8)
            for g in range(MG):
                e.eng.wait_ge(sems["cb_ready"], e.take("cb_ready"))
                nc.vector.tensor_tensor(cb[:, g, :], bank(g % 2, 0, 384), upto3, ALU.mult) \
                    .then_inc(sems["cb_masked"], e.one("cb_masked"))
            e.eng.wait_ge(sems["cb_masked"], e.own("cb_masked"))
            e.eng.wait_ge(sems[e.marked(f"x_turned_{l}")], e.reach(f"x_turned_{l}"))

            def by_head(ap):
                return ap.rearrange("p (h n) -> p h n", h=MH)
            for t in range(TT):
                ins = nc.vector.tensor_tensor(by_head(my[:, t, :]), by_head(mx[:, t, :]),
                                              row("m_d", a * MH, MH).unsqueeze(2).to_broadcast([P, MH, MP]), ALU.mult)
            ins.then_inc(sems["vector_step"], e.one("vector_step"))
            e.eng.wait_ge(sems["vector_step"], e.own("vector_step"))
            for t in range(TT):
                ins = nc.vector.tensor_tensor(by_head(mx[:, t, :]), by_head(mx[:, t, :]),
                                              m_dt[:, t, :].unsqueeze(2).to_broadcast([P, MH, MP]), ALU.mult)
            ins.then_inc(sems["inputs_scaled"], e.one("inputs_scaled"))

            def arg(h):
                e.eng.wait_ge(sems["decay_row_ready"], e.take("decay_row_ready"))
                nc.vector.tensor_scalar(m_decay[:, h % 3, 0:256], bank(2 + h % 2, 0, 256), m_sum[:, 0, h:h + 1], 0.0,
                                        ALU.subtract, ALU.min)
                nc.vector.tensor_scalar(m_decay[:, h % 3, 256:], bank(2 + h % 2, P, P), m_sum[:, 1, h:h + 1], 0.0,
                                        ALU.subtract, ALU.min) \
                    .then_inc(sems["decay_arg_ready"], e.one("decay_arg_ready"))
            arg(0)
            for h in range(MH):
                if h + 1 < MH:
                    arg(h + 1)
                e.eng.wait_ge(sems["decay_ready"], e.take("decay_ready"))
                if h >= 3:
                    e.eng.wait_ge(sems["head_done"], e.take("head_done"))
                nc.vector.tensor_tensor(m_mix[:, h % 3, :], m_decay[:, h % 3, :], cb[:, h // 4, :], ALU.mult) \
                    .then_inc(sems["mix_ready"], e.one("mix_ready"))
                if h % 8 == 0 and h:
                    heads_out(e, l, h // 8 - 1)
            heads_out(e, l, 3)
            e.eng.wait_ge(sems["head_done"], e.take("head_done", 3))
            e.eng.wait_ge(sems["roots_ready"], e.take("roots_ready"))
            nc.vector.reciprocal(m_rec, m_root).then_inc(sems["vector_step"], e.one("vector_step"))
            e.eng.wait_ge(sems["vector_step"], e.own("vector_step"))
            for half in range(2):
                for t in range(TT):
                    v = my[:, t, half * 1024:(half + 1) * 1024].rearrange("p (g n) -> p g n", n=256)
                    ins = nc.vector.tensor_tensor(v, v, m_rec[:, t, half * 4:half * 4 + 4].unsqueeze(2)
                                                  .to_broadcast([P, 4, 256]), ALU.mult)
                ins.then_inc(sems["gated_ready"], e.one("gated_ready"))
            turn_dve(e, lambda kb: yT[:, kb, :], 8, lambda kb: col("m_norm_w", a * 16 + kb))
            residual_dve(e, 8)

        def heads_out(e, l, k):
            e.eng.wait_ge(sems[e.marked(f"heads_{l}")], e.reach(f"heads_{l}", 8 * k + 8))
            for t in range(TT):
                v = my[:, t, k * 512:(k + 1) * 512]
                ins = nc.vector.tensor_tensor(v, v, bank(4 + 2 * (k % 2) + t), ALU.add)
            ins.then_inc(sems["heads_out"], e.one("heads_out"))
            e.eng.wait_ge(sems["heads_out"], e.own("heads_out"))
            for t in range(TT):
                v = my[:, t, k * 512:(k + 1) * 512]
                ins = nc.vector.tensor_tensor(v, v, mz[:, t, k * 512:(k + 1) * 512], ALU.mult)
            ins.then_inc(sems["square_sums_ready"], e.one("square_sums_ready"))

        HH, HC = 8, 32
        NCH = SEQ // HC

        def flat(buf, lo, *shape):
            n = int(np.prod(shape))
            names = "abcd"[:len(shape)]
            if len(shape) == 1:
                return buf[:, lo:lo + n]
            sizes = {k: v for k, v in zip(names, shape)}
            return buf[:, lo:lo + n].rearrange("p (%s) -> p %s" % (" ".join(names), " ".join(names)), **sizes)

        h_f = flat(bufA, 0, HH, SEQ)
        h_q = flat(bufA, 2048, HH, SEQ)
        h_g = flat(bufA, 4096, HH, SEQ)
        h_k = flat(bufA, 6144, HH, SEQ)
        h_v = flat(bufC, 0, TT, D)
        h_sum = flat(bufC, 2048, HH, SEQ)
        h_e = flat(bufE, 0, HH, SEQ)
        h_kend = flat(bufE, 2048, HH, SEQ)
        h_kt = flat(bufB, 0, TT, D)
        h_state = flat(bufB, 2048, HH, P)
        h_att = flat(bufB, 3072, HH, P)
        h_last = st[:, 128:192].rearrange("p (h c) -> p h c", h=HH)
        h_lb, h_lb1 = st[:, 192:200], st[:, 200:208]
        h_ex = st[:, 208:240].rearrange("p (l k) -> p l k", l=4)
        h_tot = st[:, 240:248]

        def hgrn_pe(e, l):
            norm_pe(e)
            project_pe(e, 12, page_wide_fm, hT)
            project_pe(e, 4, page_wide_tm, hT)
            e.eng.wait_ge(sems["projected_out"], e.ahead("projected_out", 2))
            e.eng.wait_ge(sems["kend_ready"], e.take("kend_ready"))
            turn_pe(e, lambda kb, t: h_kend[:, kb, t * P:(t + 1) * P], 4)
            e.eng.wait_ge(sems["decayed_ready"], e.take("decayed_ready"))
            e.eng.wait_ge(sems["state_cleared"], e.take("state_cleared"))
            for t in range(TT):
                tok = slice(t * P, (t + 1) * P)
                for h in range(HH):
                    ins = nc.tensor.matmul(bank(h // 4, (h % 4) * P, P), h_k[:, h, tok], h_q[:, h, tok],
                                           start=True, stop=True)
                ins.then_inc(sems["scores_ready"], e.one("scores_ready"))
                e.eng.wait_ge(sems["h_scores_masked"], e.take("h_scores_masked"))
                for h in range(HH):
                    nc.tensor.matmul(bank(4 + h // 4, (h % 4) * P, P), h_v[:, t, h * P:(h + 1) * P], h_att[:, h, :],
                                     start=h % 4 == 0, stop=False, skip_group_check=True)
                for c in range(P // HC):
                    lo = c * HC
                    for h in range(HH):
                        ins = nc.tensor.matmul(bank(4 + h // 4, (h % 4) * P + lo, HC), h_state[:, h, :],
                                               h_q[:, h, t * P + lo:t * P + lo + HC],
                                               start=False, stop=c == 3, skip_group_check=True)
                    if c == 3:
                        ins.then_inc(sems["h_out_ready"], e.one("h_out_ready"))
                    if t == TT - 1 and c == 3:
                        break
                    for h in range(HH):
                        ins = nc.tensor.matmul(bank(6 + h // 4, (h % 4) * P, P), h_kt[lo:lo + HC, t, h * P:(h + 1) * P],
                                               h_v[lo:lo + HC, t, h * P:(h + 1) * P], start=True, stop=True)
                    ins.then_inc(sems["h_added_ready"], e.one("h_added_ready"))
                    e.eng.wait_ge(sems["h_state_ready"], e.take("h_state_ready"))
                e.eng.wait_ge(sems["h_out_copied"], e.take("h_out_copied"))
            for g in range(4):
                if g >= 2:
                    e.eng.wait_ge(sems["norm_sums_read"], e.take("norm_sums_read"))
                e.eng.wait_ge(sems["squares_ready"], e.take("squares_ready"))
                for j in range(2):
                    ins = nc.tensor.matmul(bank(g % 2, j * SEQ, SEQ), ones, h_kend[:, 2 * g + j, :], start=True, stop=True)
                ins.then_inc(sems["norm_sums_ready"], e.one("norm_sums_ready"))
            e.eng.wait_ge(sems["norm_sums_read"], e.take("norm_sums_read", 2))
            e.eng.wait_ge(sems["h_gated_ready"], e.take("h_gated_ready"))
            down_pe(e, 4, lambda kb: yT[:, kb, :])

        def hgrn_act(e, l):
            normed_act(e, lambda kb: col("ln_mix", l * KB + kb))
            e.eng.wait_ge(sems["exponent_ready"], e.take("exponent_ready"))
            nc.scalar.activation(h_ex, h_ex, ACT.Exp).then_inc(sems["exponential_ready"], e.one("exponential_ready"))
            project_act(e, 4, lambda e, j, b: nc.scalar.copy(h_f[:, bass.ds(2 * j, 2), :], bank(b)))

            def silu_rows(dst):
                return lambda e, j, b: nc.scalar.activation(dst[:, 2 * j:2 * j + 2, :], bank(b), ACT.Silu)
            e.eng.wait_ge(sems["projected_out"], e.own("projected_out"))
            nc.scalar.activation(h_e, h_f, ACT.Exp, scale=-1.0) \
                .then_inc(sems["exponential_ready"], e.one("exponential_ready"))
            project_act(e, 4, silu_rows(h_q))
            e.eng.wait_ge(sems["forget_ready"], e.take("forget_ready"))
            nc.scalar.activation(h_f, h_f, ACT.Ln).then_inc(sems["log_forget_ready"], e.one("log_forget_ready"))
            project_act(e, 4, silu_rows(h_g))
            e.eng.wait_ge(sems["h_sum_ready"], e.take("h_sum_ready"))
            nc.scalar.activation(h_last, h_sum[:, :, HC - 1::HC], ACT.Exp) \
                .then_inc(sems["scalar_step"], e.one("scalar_step"))
            e.eng.wait_ge(sems["scalar_step"], e.own("scalar_step"))
            nc.scalar.activation(h_e, h_sum, ACT.Exp).then_inc(sems["h_exp_ready"], e.one("h_exp_ready"))
            e.eng.wait_ge(sems["h_qdec_ready"], e.take("h_qdec_ready"))
            nc.scalar.activation(h_e, h_sum, ACT.Exp, scale=-1.0).then_inc(sems["h_exp_ready"], e.one("h_exp_ready"))
            e.eng.wait_ge(sems["h_rest_ready"], e.take("h_rest_ready"))
            nc.scalar.activation(h_kend, h_kend, ACT.Exp).then_inc(sems["h_exp_ready"], e.one("h_exp_ready"))
            project_act(e, 4, lambda e, j, b: nc.scalar.copy(h_v[:, :, j * 256:(j + 1) * 256], bank(b)))
            turn_act(e, lambda kb: h_kt[:, :, kb * P:(kb + 1) * P], 4)
            for t in range(TT):
                e.eng.wait_ge(sems["h_out_ready"], e.take("h_out_ready"))
                for b in range(2):
                    ins = nc.scalar.copy(yT[:, 4 * b:4 * b + 4, t * P:(t + 1) * P],
                                         bank(4 + b).rearrange("p (h s) -> p h s", h=4))
                ins.then_inc(sems["h_out_copied"], e.one("h_out_copied"))
            e.eng.wait_ge(sems["h_out_copied"], e.own("h_out_copied"))
            for g in range(4):
                nc.scalar.activation(h_kend[:, 2 * g:2 * g + 2, :], yT[:, 2 * g:2 * g + 2, :], ACT.Square) \
                    .then_inc(sems["squares_ready"], e.one("squares_ready"))
            for g in range(4):
                e.eng.wait_ge(sems["norm_sums_ready"], e.take("norm_sums_ready"))
                nc.scalar.activation(h_e[:, 2 * g:2 * g + 2, :], bank(g % 2), ACT.Sqrt, bias=const("eps", 0, 1),
                                     scale=1.0 / P).then_inc(sems["norm_sums_read"], e.one("norm_sums_read"))
            e.page += 4

        def hgrn_dve(e, l):
            normed_dve(e, lambda kb: col("ln_mix", l * KB + kb))
            logits = cols[:, COL_AT["h_lower_bounds"]:COL_AT["h_lower_bounds"] + 32].rearrange("p (l k) -> p l k", l=4)
            nc.vector.tensor_tensor(h_tot, logits[:, 0, :], logits[:, 1, :], ALU.max) \
               .then_inc(sems["vector_step"], e.one("vector_step"))
            e.eng.wait_ge(sems["vector_step"], e.own("vector_step"))
            nc.vector.tensor_tensor(h_tot, h_tot, logits[:, 2, :], ALU.max) \
               .then_inc(sems["vector_step"], e.one("vector_step"))
            e.eng.wait_ge(sems["vector_step"], e.own("vector_step"))
            nc.vector.tensor_tensor(h_tot, h_tot, logits[:, 3, :], ALU.max) \
               .then_inc(sems["vector_step"], e.one("vector_step"))
            e.eng.wait_ge(sems["vector_step"], e.own("vector_step"))
            nc.vector.tensor_tensor(h_ex, logits, h_tot.unsqueeze(1).to_broadcast([P, 4, KB]), ALU.subtract) \
                .then_inc(sems["exponent_ready"], e.one("exponent_ready"))
            e.eng.wait_ge(sems["exponential_ready"], e.take("exponential_ready"))
            nc.vector.tensor_tensor(h_tot, h_ex[:, 0, :], h_ex[:, 1, :], ALU.add) \
               .then_inc(sems["vector_step"], e.one("vector_step"))
            e.eng.wait_ge(sems["vector_step"], e.own("vector_step"))
            nc.vector.tensor_tensor(h_tot, h_tot, h_ex[:, 2, :], ALU.add) \
               .then_inc(sems["vector_step"], e.one("vector_step"))
            e.eng.wait_ge(sems["vector_step"], e.own("vector_step"))
            nc.vector.tensor_tensor(h_tot, h_tot, h_ex[:, 3, :], ALU.add) \
               .then_inc(sems["vector_step"], e.one("vector_step"))
            e.eng.wait_ge(sems["vector_step"], e.own("vector_step"))
            nc.vector.reciprocal(h_tot, h_tot).then_inc(sems["vector_step"], e.one("vector_step"))
            e.eng.wait_ge(sems["vector_step"], e.own("vector_step"))
            nc.vector.tensor_tensor(h_lb, h_ex[:, 1, :], h_tot, ALU.mult) \
               .then_inc(sems["vector_step"], e.one("vector_step"))
            e.eng.wait_ge(sems["vector_step"], e.own("vector_step"))
            nc.vector.tensor_scalar(h_lb1, h_lb, -1.0, 1.0, ALU.mult, ALU.add) \
               .then_inc(sems["vector_step"], e.one("vector_step"))
            e.eng.wait_ge(sems["vector_step"], e.own("vector_step"))
            e.page += 16
            e.eng.wait_ge(sems["exponential_ready"], e.take("exponential_ready"))
            nc.vector.tensor_scalar(h_e, h_e, 1.0, None, ALU.add).then_inc(sems["vector_step"], e.one("vector_step"))
            e.eng.wait_ge(sems["vector_step"], e.own("vector_step"))
            nc.vector.reciprocal(h_e, h_e).then_inc(sems["vector_step"], e.one("vector_step"))
            e.eng.wait_ge(sems["vector_step"], e.own("vector_step"))
            for kb in range(KB):
                ins = nc.vector.tensor_scalar(h_f[:, kb, :], h_e[:, kb, :], h_lb1[:, kb:kb + 1], h_lb[:, kb:kb + 1],
                                              ALU.mult, ALU.add)
            ins.then_inc(sems["vector_step"], e.one("vector_step"))
            e.eng.wait_ge(sems["vector_step"], e.own("vector_step"))
            nc.vector.tensor_scalar(h_k, h_f, -1.0, 1.0, ALU.mult, ALU.add) \
                .then_inc(sems["forget_ready"], e.one("forget_ready"))
            e.eng.wait_ge(sems["log_forget_ready"], e.take("log_forget_ready"))
            for kb in range(KB):
                ins = nc.vector.tensor_tensor_scan(h_sum[:, kb, :], const("restart32"), h_f[:, kb, :], 0.0,
                                                   ALU.mult, ALU.add)
            ins.then_inc(sems["h_sum_ready"], e.one("h_sum_ready"))
            e.eng.wait_ge(sems["h_sum_ready"], e.own("h_sum_ready"))
            for kb in range(KB):
                v = h_sum[:, kb, :].rearrange("p (c s) -> p c s", c=NCH)
                ins = nc.vector.tensor_tensor(h_kend[:, kb, :].rearrange("p (c s) -> p c s", c=NCH),
                                              v[:, :, HC - 1:HC].to_broadcast([P, NCH, HC]), v, ALU.subtract)
            ins.then_inc(sems["h_rest_ready"], e.one("h_rest_ready"))
            e.eng.wait_ge(sems["h_exp_ready"], e.take("h_exp_ready"))
            nc.vector.scalar_tensor_tensor(h_q, h_q, float(P) ** -0.5, h_e, ALU.mult, ALU.mult) \
                .then_inc(sems["h_qdec_ready"], e.one("h_qdec_ready"))
            e.eng.wait_ge(sems["h_exp_ready"], e.take("h_exp_ready", 2))
            nc.vector.tensor_tensor(h_kend, h_kend, h_k, ALU.mult).then_inc(sems["kend_ready"], e.one("kend_ready"))
            e.eng.wait_ge(sems["kend_ready"], e.own("kend_ready"))
            nc.vector.tensor_tensor(h_k, h_k, h_e, ALU.mult).then_inc(sems["decayed_ready"], e.one("decayed_ready"))
            nc.vector.memset(h_state, 0.0).then_inc(sems["state_cleared"], e.one("state_cleared"))
            turn_dve(e, lambda kb: h_kt[:, :, kb * P:(kb + 1) * P], 4)
            gla = const("gla").unsqueeze(1).to_broadcast([P, 4, P])
            for t in range(TT):
                e.eng.wait_ge(sems["scores_ready"], e.take("scores_ready"))
                for b in range(2):
                    ins = nc.vector.tensor_scalar(h_att[:, 4 * b:4 * b + 4, :], bank(b).rearrange("p (h s) -> p h s", h=4),
                                                  3.0e38, -3.0e38, ALU.min, ALU.max)
                ins.then_inc(sems["vector_step"], e.one("vector_step"))
                e.eng.wait_ge(sems["vector_step"], e.own("vector_step"))
                for b in range(2):
                    v = h_att[:, 4 * b:4 * b + 4, :]
                    ins = nc.vector.tensor_tensor(v, v, gla, ALU.mult)
                ins.then_inc(sems["h_scores_masked"], e.one("h_scores_masked"))
                for c in range(P // HC):
                    if t == TT - 1 and c == 3:
                        break
                    e.eng.wait_ge(sems["h_added_ready"], e.take("h_added_ready"))
                    for h in range(HH):
                        ch = t * 4 + c
                        ins = nc.vector.scalar_tensor_tensor(h_state[:, h, :], h_state[:, h, :], h_last[:, h, ch:ch + 1],
                                                             bank(6 + h // 4, (h % 4) * P, P), ALU.mult, ALU.add)
                    ins.then_inc(sems["h_state_ready"], e.one("h_state_ready"))
                    e.eng.wait_ge(sems["h_state_ready"], e.own("h_state_ready"))
            for g in range(4):
                e.eng.wait_ge(sems["norm_sums_read"], e.take("norm_sums_read"))
                v, r = yT[:, 2 * g:2 * g + 2, :], h_e[:, 2 * g:2 * g + 2, :]
                nc.vector.reciprocal(r, r).then_inc(sems["vector_step"], e.one("vector_step"))
                e.eng.wait_ge(sems["vector_step"], e.own("vector_step"))
                nc.vector.scalar_tensor_tensor(v, v, col("h_norm_w", 0), r, ALU.mult, ALU.mult) \
                   .then_inc(sems["vector_step"], e.one("vector_step"))
                e.eng.wait_ge(sems["vector_step"], e.own("vector_step"))
                ins = nc.vector.tensor_tensor(v, v, h_g[:, 2 * g:2 * g + 2, :], ALU.mult)
            ins.then_inc(sems["h_gated_ready"], e.one("h_gated_ready"))
            residual_dve(e, 4)

        LEVELS = 7

        def quad(ap):
            return ap.rearrange("p (m s) -> p m s", m=4)

        def over4(c):
            return c.unsqueeze(1).to_broadcast([P, 4, P])

        def invert_pe(e, T, Tt, Mb, P1):
            for lev in range(1, LEVELS):
                for z in range(2):
                    e.eng.wait_ge(sems["joint_ready"], e.take("joint_ready"))
                    for m in range(4):
                        ins = nc.tensor.matmul(bank(z, m * P, P), Mb[z][:, m, :], T[z][:, m, :], start=True, stop=True)
                    ins.then_inc(sems["joint_product_ready"], e.one("joint_product_ready"))
                for z in range(2):
                    e.eng.wait_ge(sems["joint_product_out"], e.take("joint_product_out"))
                    if lev < LEVELS - 1:
                        for m in range(4):
                            nc.tensor.matmul(bank(2 + z, m * P, P), Tt[z][:, m, :], P1[z][:, m, :], start=True, stop=True)
                    for m in range(4):
                        ins = nc.tensor.matmul(bank(4 + z, m * P, P), P1[z][:, m, :], Tt[z][:, m, :], start=True, stop=True)
                    ins.then_inc(sems["join_ready"], e.one("join_ready"))
            e.eng.wait_ge(sems["inverse_ready"], e.take("inverse_ready", 2))

        def invert_act(e, P1):
            for lev in range(1, LEVELS):
                for z in range(2):
                    e.eng.wait_ge(sems["joint_product_ready"], e.take("joint_product_ready"))
                    nc.scalar.copy(P1[z], quad(bank(z))) \
                        .then_inc(sems["joint_product_out"], e.one("joint_product_out"))

        def invert_dve(e, T, Tt, MT, Mb):
            for z in range(2):
                nc.vector.tensor_tensor(T[z], T[z], over4(const("join1")), ALU.mult)
                nc.vector.tensor_tensor(Tt[z], MT[z], over4(const("join_t", 0, P)), ALU.mult) \
                   .then_inc(sems["vector_step"], e.one("vector_step"))
                e.eng.wait_ge(sems["vector_step"], e.own("vector_step"))
                nc.vector.scalar_tensor_tensor(T[z], T[z], -1.0, over4(ident), ALU.mult, ALU.add)
                nc.vector.scalar_tensor_tensor(Tt[z], Tt[z], -1.0, over4(ident), ALU.mult, ALU.add)
                nc.vector.tensor_tensor(Mb[z], MT[z], over4(const("join_t", P, P)), ALU.mult) \
                    .then_inc(sems["joint_ready"], e.one("joint_ready"))
            for lev in range(1, LEVELS):
                for z in range(2):
                    e.eng.wait_ge(sems["join_ready"], e.take("join_ready"))
                    if lev < LEVELS - 1:
                        nc.vector.tensor_tensor(T[z], T[z], quad(bank(2 + z)), ALU.subtract)
                        nc.vector.tensor_tensor(Tt[z], Tt[z], quad(bank(4 + z)), ALU.subtract)
                        nc.vector.tensor_tensor(Mb[z], MT[z], over4(const("join_t", (lev + 1) * P, P)), ALU.mult) \
                            .then_inc(sems["joint_ready"], e.one("joint_ready"))
                        e.eng.wait_ge(sems["joint_ready"], e.own("joint_ready"))
                    else:
                        nc.vector.tensor_tensor(Tt[z], Tt[z], quad(bank(4 + z)), ALU.subtract) \
                            .then_inc(sems["inverse_ready"], e.one("inverse_ready"))

        GH = 16
        g_qT = flat(bufA, 0, 8, PADW)
        g_kT = flat(bufA, 8 * PADW, 8, PADW)
        g_z = flat(bufB, 0, TT, 2048)
        g_v = flat(bufC, 0, TT, 2048)
        g_o = flat(bufE, 0, TT, 2048)
        hflat = hT[:, :, :].rearrange("p k s -> p (k s)")
        g_kt = flat(hflat, 0, D)
        g_r = flat(hflat, 1024, 4, P)
        g_s = flat(hflat, 1536, 4, P)

        def pair(buf, lo):
            return [flat(buf, lo + 512 * z, 4, P) for z in range(2)]

        A_FREE = 16 * PADW
        g_dec, g_att, g_m = pair(yflat, 0), pair(yflat, 1024), pair(yflat, 2048)
        g_mt, g_attT, g_tt = pair(yflat, 3072), pair(bufA, A_FREE), pair(bufA, A_FREE + 1024)
        g_new = [flat(bufA, A_FREE + 2048 + 512 * k, 4, P) for k in range(3)]
        g_rows = bufA[:, A_FREE + 3584:A_FREE + 3584 + SEQ]
        g_beta, g_g, g_sum, g_eg, g_t1, g_rb = (s2(128 + 32 * k, GH) for k in range(6))
        g_a, g_tot, g_el, g_ek = (st[:, 320 + 16 * k:336 + 16 * k] for k in range(4))
        g_ss, g_root, g_rec = s2(400, GH), s2(432, GH), s2(464, GH)
        g_sq = flat(bufE, 0, 2, 2, SEQ)
        g_nrm = flat(bufE, 1024, 2, 2, SEQ)

        def gdn_pe(e, l):
            norm_pe(e)
            narrow_pe(e, small("g_ba_w"), 4, 32, "narrow_ready")
            project_pe(e, 16, page_wide_fm, hT)
            project_pe(e, 8, page_wide_tm, hT)
            e.eng.wait_ge(sems["step_decays_ready"], e.take("step_decays_ready"))
            nc.tensor.matmul(bank(5, 0, 2 * GH), upto, st[:, 160:192], start=True, stop=True)
            nc.tensor.matmul(bank(5, 64, GH), ones, g_g[:, 0, :], start=True, stop=True)
            for t in range(TT):
                ins = nc.tensor.matmul(bank(5, 128 + t * P, P)[0:GH, :], g_g[:, t, :], upto, start=True, stop=True)
            ins.then_inc(sems["sums_ready"], e.one("sums_ready"))
            e.eng.wait_ge(sems["projected_out"], e.ahead("projected_out", 2))
            for c in range(8):
                e.eng.wait_ge(sems["squares_ready"], e.take("squares_ready"))
                if c >= 2:
                    e.eng.wait_ge(sems["norm_sums_read"], e.take("norm_sums_read"))
                for j in range(2):
                    ins = nc.tensor.matmul(bank(c % 2, j * SEQ, SEQ), ones, g_sq[:, c % 2, j, :], start=True, stop=True)
                ins.then_inc(sems["norm_sums_ready"], e.one("norm_sums_ready"))
            e.eng.wait_ge(sems["norm_sums_read"], e.take("norm_sums_read", 2))
            turn_pe(e, lambda c, t: conved[:, 16 + c, CW - 1 + t * P:CW - 1 + (t + 1) * P], 8)
            e.eng.wait_ge(sems["g_heads_normed"], e.take("g_heads_normed"))
            for c in range(8):
                ins = nc.tensor.transpose(bank(c // 4, (c % 4) * P, P), g_kT[:, c, CW - 1:CW - 1 + P], ident)
            ins.then_inc(sems["g_keys_turned"], e.one("g_keys_turned"))
            e.eng.wait_ge(sems["g_inputs_ready"], e.take("g_inputs_ready"))
            for b in range(4):
                group_pe(e, b)
            e.eng.wait_ge(sems["gated_ready"], e.take("gated_ready"))
            turn_pe(e, lambda kb, t: g_o[:, t, kb * P:(kb + 1) * P], 8)
            down_pe(e, 8, lambda kb: yT[:, kb, :])

        def tokens_of(ap, z):
            return ap[:, CW - 1 + z * P:CW - 1 + (z + 1) * P]

        def group_pe(e, b):
            for z in range(2):
                for j in range(2):
                    k, q = tokens_of(g_kT[:, 2 * b + j, :], z), tokens_of(g_qT[:, 2 * b + j, :], z)
                    nc.tensor.matmul(bank(0, (2 * z + j) * P, P), k, k, start=True, stop=True)
                    nc.tensor.matmul(bank(1, (2 * z + j) * P, P), q, k, start=True, stop=True)
                for m in range(4):
                    h = 4 * b + m
                    ins = nc.tensor.matmul(bank(2 + z, m * P, P), ident[0:GH, h:h + 1].to_broadcast([GH, P]),
                                           g_rows[0:GH, z * P:(z + 1) * P], start=True, stop=True)
            ins.then_inc(sems["g_grams_ready"], e.one("g_grams_ready"))
            for z in range(2):
                e.eng.wait_ge(sems["g_matrices_ready"], e.take("g_matrices_ready"))
                for m in range(4):
                    nc.tensor.transpose(bank(4 + z, m * P, P), g_m[z][:, m, :], ident)
                for m in range(4):
                    ins = nc.tensor.transpose(bank(6 + z, m * P, P), g_att[z][:, m, :], ident)
                ins.then_inc(sems["g_matrices_turned"], e.one("g_matrices_turned"))
            invert_pe(e, g_m, g_tt, g_att, g_dec)
            heads = range(4)

            def vcols(m):
                return slice((4 * b + m) * P, (4 * b + m + 1) * P)
            for m in heads:
                ins = nc.tensor.matmul(bank(6, m * P, P), g_tt[0][:, m, :], g_v[:, 0, vcols(m)], start=True, stop=True)
            ins.then_inc(sems["g_new_ready"], e.one("g_new_ready"))
            e.eng.wait_ge(sems["g_new_out"], e.take("g_new_out"))
            for m in heads:
                ins = nc.tensor.matmul(bank(7, m * P, P), g_attT[0][:, m, :], g_new[0][:, m, :], start=True, stop=True)
            ins.then_inc(sems["g_out0_ready"], e.one("g_out0_ready"))
            e.eng.wait_ge(sems["g_new_decayed"], e.take("g_new_decayed"))
            for m in heads:
                kc = (2 * b + m // 2) * P
                ins = nc.tensor.matmul(bank(0, m * P, P), g_kt[:, kc:kc + P], g_new[1][:, m, :], start=True, stop=True)
            ins.then_inc(sems["g_state_ready"], e.one("g_state_ready"))
            e.eng.wait_ge(sems["g_state_out"], e.take("g_state_out"))
            for m in heads:
                nc.tensor.matmul(bank(1, m * P, P), tokens_of(g_kT[:, 2 * b + m // 2, :], 1), g_s[:, m, :], start=True, stop=True)
            for m in heads:
                ins = nc.tensor.matmul(bank(2, m * P, P), tokens_of(g_qT[:, 2 * b + m // 2, :], 1), g_s[:, m, :],
                                       start=True, stop=True)
            ins.then_inc(sems["g_from_state_ready"], e.one("g_from_state_ready"))
            e.eng.wait_ge(sems["g_rhs_ready"], e.take("g_rhs_ready"))
            for m in heads:
                ins = nc.tensor.matmul(bank(3, m * P, P), g_tt[1][:, m, :], g_r[:, m, :], start=True, stop=True)
            ins.then_inc(sems["g_new_ready"], e.one("g_new_ready"))
            e.eng.wait_ge(sems["g_new_out"], e.take("g_new_out"))
            for m in heads:
                ins = nc.tensor.matmul(bank(4, m * P, P), g_attT[1][:, m, :], g_new[2][:, m, :], start=True, stop=True)
            ins.then_inc(sems["g_out1_ready"], e.one("g_out1_ready"))
            e.eng.wait_ge(sems["g_group_done"], e.take("g_group_done"))

        def gdn_act(e, l):
            normed_act(e, lambda kb: col("ln_mix", l * KB + kb))
            nc.scalar.activation(g_a, row("g_a_log"), ACT.Exp).then_inc(sems["rates_ready"], e.one("rates_ready"))
            e.eng.wait_ge(sems["exponent_ready"], e.take("exponent_ready"))
            nc.scalar.activation(g_beta, g_beta, ACT.Exp, scale=-1.0) \
                .then_inc(sems["exponential_ready"], e.one("exponential_ready"))
            softplus_act(e, g_t1)
            conv_project_act(e, 16)
            project_act(e, 8, silu_columns(g_z))
            for c in range(8):
                if c >= 2:
                    e.eng.wait_ge(sems["g_norm_used"], e.take("g_norm_used"))
                src = conved[:, 2 * c:2 * c + 2, CW - 1:]
                nc.scalar.activation(g_sq[:, c % 2, :, :], src, ACT.Square) \
                    .then_inc(sems["squares_ready"], e.one("squares_ready"))
                e.eng.wait_ge(sems["norm_sums_ready"], e.take("norm_sums_ready"))
                nc.scalar.activation(g_nrm[:, c % 2, :, :], bank(c % 2).rearrange("p (m s) -> p m s", m=2),
                                     ACT.Sqrt, bias=const("eps", 0, 1)) \
                    .then_inc(sems["norm_sums_read"], e.one("norm_sums_read"))
            turn_act(e, lambda c: g_v[:, :, c * P:(c + 1) * P], 8)
            e.mark("g_values_turned", "turned_out_act")
            e.eng.wait_ge(sems["g_keys_turned"], e.take("g_keys_turned"))
            for k in range(2):
                ins = nc.scalar.copy(g_kt[:, 512 * k:512 * k + 512], bank(k))
            ins.then_inc(sems["g_keys_out"], e.one("g_keys_out"))
            e.eng.wait_ge(sems["g_decay_arg_ready"], e.take("g_decay_arg_ready"))
            nc.scalar.activation(g_eg, g_sum, ACT.Exp)
            nc.scalar.activation(g_el, g_tot, ACT.Exp)
            nc.scalar.activation(g_ek, g_ek, ACT.Exp).then_inc(sems["g_decays_ready"], e.one("g_decays_ready"))
            for b in range(4):
                for z in range(2):
                    e.eng.wait_ge(sems["g_arg_ready"], e.take("g_arg_ready"))
                    nc.scalar.activation(g_dec[z], g_dec[z], ACT.Exp, scale=-1.0) \
                        .then_inc(sems["g_dec_ready"], e.one("g_dec_ready"))
                for z in range(2):
                    e.eng.wait_ge(sems["g_matrices_turned"], e.take("g_matrices_turned"))
                    nc.scalar.copy(g_mt[z], quad(bank(4 + z)))
                    nc.scalar.copy(g_attT[z], quad(bank(6 + z))).then_inc(sems["g_turned_out"], e.one("g_turned_out"))
                invert_act(e, g_dec)
                e.eng.wait_ge(sems["g_new_ready"], e.take("g_new_ready"))
                nc.scalar.copy(g_new[0], quad(bank(6))).then_inc(sems["g_new_out"], e.one("g_new_out"))
                e.eng.wait_ge(sems["g_out0_ready"], e.take("g_out0_ready"))
                nc.scalar.copy(g_o[:, 0, b * 512:(b + 1) * 512], bank(7))
                e.eng.wait_ge(sems["g_state_ready"], e.take("g_state_ready"))
                nc.scalar.copy(g_s, quad(bank(0))).then_inc(sems["g_state_out"], e.one("g_state_out"))
                e.eng.wait_ge(sems["g_new_ready"], e.take("g_new_ready"))
                nc.scalar.copy(g_new[2], quad(bank(3))).then_inc(sems["g_new_out"], e.one("g_new_out"))
                e.eng.wait_ge(sems["g_out1_ready"], e.take("g_out1_ready"))
                nc.scalar.copy(g_o[:, 1, b * 512:(b + 1) * 512], bank(4)) \
                    .then_inc(sems["g_out_copied"], e.one("g_out_copied"))
            group_norm_root_act(e, g_root, g_ss, P)
            turn_act(e, lambda kb: yT[:, kb, :], 8, lambda kb: col("g_norm_w", 0))
            e.page += 8

        def gdn_dve(e, l):
            normed_dve(e, lambda kb: col("ln_mix", l * KB + kb))
            e.eng.wait_ge(sems["narrow_ready"], e.take("narrow_ready"))
            for t in range(TT):
                nc.vector.tensor_copy(g_beta[:, t, :], bank(4, 64 * t, GH))
                ins = nc.vector.tensor_tensor(g_rb[:, t, :], bank(4, 64 * t + GH, GH), row("g_dt_bias"), ALU.add)
            ins.then_inc(sems["exponent_ready"], e.one("exponent_ready"))
            e.eng.wait_ge(sems["exponent_ready"], e.own("exponent_ready"))
            softplus_dve(e, g_rb, g_t1)
            e.eng.wait_ge(sems["exponential_ready"], e.take("exponential_ready"))
            nc.vector.tensor_scalar(g_beta, g_beta, 1.0, None, ALU.add) \
               .then_inc(sems["vector_step"], e.one("vector_step"))
            e.eng.wait_ge(sems["vector_step"], e.own("vector_step"))
            nc.vector.reciprocal(g_beta, g_beta).then_inc(sems["vector_step"], e.one("vector_step"))
            e.eng.wait_ge(sems["vector_step"], e.own("vector_step"))
            e.eng.wait_ge(sems["rates_ready"], e.take("rates_ready"))
            nc.vector.scalar_tensor_tensor(g_g, g_rb, -1.0, g_a.unsqueeze(1).to_broadcast([P, TT, GH]),
                                           ALU.mult, ALU.mult) \
                .then_inc(sems["step_decays_ready"], e.one("step_decays_ready"))
            conv_project_dve(e, 16, lambda tap, c: col("g_conv_w", c + tap * 32), None)
            e.page += 24
            e.eng.wait_ge(sems["sums_ready"], e.take("sums_ready"))
            nc.vector.tensor_copy(g_sum, bank(5, 0, 2 * GH).rearrange("p (t n) -> p t n", t=TT))
            nc.vector.tensor_copy(g_tot, bank(5, 64, GH)).then_inc(sems["vector_step"], e.one("vector_step"))
            e.eng.wait_ge(sems["vector_step"], e.own("vector_step"))
            nc.vector.tensor_tensor(g_ek, g_tot, g_sum[:, 0, :], ALU.subtract) \
                .then_inc(sems["g_decay_arg_ready"], e.one("g_decay_arg_ready"))
            for c in range(8):
                e.eng.wait_ge(sems["norm_sums_read"], e.take("norm_sums_read"))
                nc.vector.reciprocal(g_nrm[:, c % 2, :, :], g_nrm[:, c % 2, :, :]) \
                   .then_inc(sems["vector_step"], e.one("vector_step"))
                e.eng.wait_ge(sems["vector_step"], e.own("vector_step"))
                v = conved[:, 2 * c:2 * c + 2, CW - 1:]
                nc.vector.scalar_tensor_tensor(v, v, float(P) ** -0.5 if c < 4 else 1.0, g_nrm[:, c % 2, :, :],
                                               ALU.mult, ALU.mult).then_inc(sems["g_norm_used"], e.one("g_norm_used"))
            turn_dve(e, lambda c: g_v[:, :, c * P:(c + 1) * P], 8)
            nc.vector.tensor_copy(g_rows[0:GH, :], bank(5, 128, SEQ)[0:GH, :]) \
                .then_inc(sems["g_heads_normed"], e.one("g_heads_normed"))
            e.eng.wait_ge(sems["g_heads_normed"], e.own("g_heads_normed"))
            e.eng.wait_ge(sems[e.marked("g_values_turned")], e.reach("g_values_turned"))
            for t in range(TT):
                v = g_v[:, t, :].rearrange("p (h n) -> p h n", h=GH)
                ins = nc.vector.tensor_tensor(v, v, g_beta[:, t, :].unsqueeze(2).to_broadcast([P, GH, P]), ALU.mult)
            ins.then_inc(sems["vector_step"], e.one("vector_step"))
            e.eng.wait_ge(sems["vector_step"], e.own("vector_step"))
            e.eng.wait_ge(sems["g_decays_ready"], e.take("g_decays_ready"))
            e.eng.wait_ge(sems["g_keys_out"], e.take("g_keys_out"))
            nc.vector.scalar_tensor_tensor(g_t1, g_beta, -1.0, g_eg, ALU.mult, ALU.mult) \
                .then_inc(sems["g_inputs_ready"], e.one("g_inputs_ready"))
            e.eng.wait_ge(sems["g_inputs_ready"], e.own("g_inputs_ready"))
            for b in range(4):
                e.eng.wait_ge(sems["g_grams_ready"], e.take("g_grams_ready"))
                for z in range(2):
                    for m in range(4):
                        h = 4 * b + m
                        ins = nc.vector.tensor_scalar(g_dec[z][:, m, :], bank(2 + z, m * P, P), g_sum[:, z, h:h + 1], 0.0,
                                                      ALU.subtract, ALU.max)
                    ins.then_inc(sems["g_arg_ready"], e.one("g_arg_ready"))
                for z in range(2):
                    e.eng.wait_ge(sems["g_dec_ready"], e.take("g_dec_ready"))
                    nc.vector.tensor_tensor(g_dec[z], g_dec[z], over4(const("since")), ALU.mult) \
                       .then_inc(sems["vector_step"], e.one("vector_step"))
                    e.eng.wait_ge(sems["vector_step"], e.own("vector_step"))
                    for j in range(2):
                        nc.vector.tensor_tensor(g_att[z][:, 2 * j:2 * j + 2, :], g_dec[z][:, 2 * j:2 * j + 2, :],
                                                bank(1, (2 * z + j) * P, P).unsqueeze(1).to_broadcast([P, 2, P]), ALU.mult)
                        for m in (2 * j, 2 * j + 1):
                            h = 4 * b + m
                            ins = nc.vector.scalar_tensor_tensor(g_m[z][:, m, :], g_dec[z][:, m, :], g_beta[:, z, h:h + 1],
                                                                 bank(0, (2 * z + j) * P, P), ALU.mult, ALU.mult)
                    ins.then_inc(sems["vector_step"], e.one("vector_step"))
                    e.eng.wait_ge(sems["vector_step"], e.own("vector_step"))
                    nc.vector.tensor_tensor(g_m[z], g_m[z], over4(const("after")), ALU.mult) \
                        .then_inc(sems["g_matrices_ready"], e.one("g_matrices_ready"))
                    e.eng.wait_ge(sems["g_matrices_ready"], e.own("g_matrices_ready"))
                e.eng.wait_ge(sems["g_turned_out"], e.take("g_turned_out", 2))
                invert_dve(e, g_m, g_tt, g_mt, g_att)
                e.eng.wait_ge(sems["g_new_out"], e.take("g_new_out"))
                for m in range(4):
                    h = 4 * b + m
                    ins = nc.vector.tensor_scalar(g_new[1][:, m, :], g_new[0][:, m, :], g_ek[:, h:h + 1], None, ALU.mult)
                ins.then_inc(sems["g_new_decayed"], e.one("g_new_decayed"))
                e.eng.wait_ge(sems["g_from_state_ready"], e.take("g_from_state_ready"))
                for m in range(4):
                    h = 4 * b + m
                    ins = nc.vector.scalar_tensor_tensor(g_r[:, m, :], bank(1, m * P, P), g_t1[:, 1, h:h + 1],
                                                         g_v[:, 1, h * P:(h + 1) * P], ALU.mult, ALU.add)
                ins.then_inc(sems["g_rhs_ready"], e.one("g_rhs_ready"))
                e.eng.wait_ge(sems["g_new_out"], e.take("g_new_out"))
                e.eng.wait_ge(sems["g_out_copied"], e.take("g_out_copied"))
                for m in range(4):
                    h = 4 * b + m
                    v = g_o[:, 1, h * P:(h + 1) * P]
                    ins = nc.vector.scalar_tensor_tensor(v, bank(2, m * P, P), g_eg[:, 1, h:h + 1], v, ALU.mult, ALU.add)
                ins.then_inc(sems["g_group_done"], e.one("g_group_done"))
            e.eng.wait_ge(sems["g_group_done"], e.own("g_group_done"))
            group_scale_dve(e, g_o, g_v, g_ss, g_root, g_rec, P).then_inc(sems["vector_step"], e.one("vector_step"))
            e.eng.wait_ge(sems["vector_step"], e.own("vector_step"))
            nc.vector.tensor_tensor(g_o, g_o, g_z, ALU.mult).then_inc(sems["gated_ready"], e.one("gated_ready"))
            turn_dve(e, lambda kb: yT[:, kb, :], 8, lambda kb: col("g_norm_w", 0))
            residual_dve(e, 8)

        RW = 512
        PR = SEQ + 1
        r_raw = flat(bufA, 0, 14, PR)
        r_x = flat(yflat, 0, 14, SEQ)
        r_a, r_lw, r_gc, r_kk = (flat(bufA, 1024 * k, 4, SEQ) for k in range(4))
        r_al, r_bh, r_kh, r_rh = (flat(bufA, 4096 + 1024 * k, 4, SEQ) for k in range(4))
        r_v, r_y, r_gate = (flat(bufE, 1024 * k, TT, RW) for k in range(3))
        r_bt, r_kt = flat(bufE, 3072, RW), flat(bufE, 3584, RW)
        d_qkv = flat(bufC, 0, TT, 3 * RW)
        x_gates = flat(bufB, 0, TT, 2048)
        r_t = flat(hflat, 0, 2, 4, SEQ)
        r_p1, r_mb, r_m, r_mt = (pair(bufA, 1024 * k) for k in range(4))
        r_tt, r_nt, r_rb, r_rk = (pair(yflat, 1024 * k) for k in range(4))
        r_rhs, r_u = flat(hflat, 0, 4, 64), flat(hflat, 256, 4, 64)
        r_s = flat(hflat, 512, 4, 64)
        r_end = st[:, 128:132]
        r_bonus = s2(136, 8)
        r_mean, r_ss, r_root, r_rec = (s2(152 + 16 * k, 8) for k in range(4))
        RC = float(np.exp(-0.5))

        def columns(name, n):
            at = COL_AT[name]
            return cols[:, at:at + n].unsqueeze(2).to_broadcast([P, n, SEQ])

        def half(m):
            return slice((m % 2) * 64, (m % 2) * 64 + 64)

        def mixtwo_pe(e, l):
            norm_pe(e)
            project_pe(e, 7, page_wide_fm, hT)
            project_pe(e, 14, page_wide_tm, hT, phase=1)
            e.eng.wait_ge(sems["lora_in_ready"], e.take("lora_in_ready"))
            lora, gw = small("lora_w"), small("gate_w")
            for c in range(4):
                nc.tensor.matmul(bank(4 + c // 2, (c % 2) * 256, 256), lora[0:64, c * P:(c + 1) * P],
                                 r_x[0:64, 12, :], start=True, stop=True)
                ins = nc.tensor.matmul(bank(6 + c // 2, (c % 2) * 256, 256), lora[64:P, c * P:(c + 1) * P],
                                       r_x[64:P, 12, :], start=True, stop=True)
            ins.then_inc(sems["lora_ready"], e.one("lora_ready"))
            e.eng.wait_ge(sems["projected_out"], e.ahead("projected_out", 2))
            for t in range(TT):
                ins = nc.tensor.matmul(bank(t), r_x[:, 13, t * P:(t + 1) * P], gw, start=True, stop=True)
            ins.then_inc(sems["r_gate_ready"], e.one("r_gate_ready"))
            e.eng.wait_ge(sems["r_gate_out"], e.take("r_gate_out"))
            e.eng.wait_ge(sems["r_squares_ready"], e.take("r_squares_ready"))
            for c in range(4):
                ins = nc.tensor.matmul(bank(c // 2, (c % 2) * 256, 256), const("blk64"), r_t[:, 0, c, :],
                                       start=True, stop=True)
            ins.then_inc(sems["r_norm_ready"], e.one("r_norm_ready"))
            turn_pe(e, lambda c, t: r_x[:, 8 + c, t * P:(t + 1) * P], 2)
            e.eng.wait_ge(sems["r_bonus_in_ready"], e.take("r_bonus_in_ready"))
            for t in range(TT):
                for c in range(4):
                    ins = nc.tensor.matmul(bank(4, 16 * t + 2 * c, 2), r_t[:, 1, c, t * P:(t + 1) * P], const("half2"),
                                           start=True, stop=True)
            ins.then_inc(sems["r_bonus_ready"], e.one("r_bonus_ready"))
            e.eng.wait_ge(sems["r_factors_ready"], e.take("r_factors_ready"))
            for c in range(4):
                nc.tensor.transpose(bank(5, c * P, P), r_bh[:, c, 0:P], ident)
                ins = nc.tensor.transpose(bank(6, c * P, P), r_kh[:, c, 0:P], ident)
            ins.then_inc(sems["r_first_turned"], e.one("r_first_turned"))
            e.eng.wait_ge(sems["r_first_out"], e.take("r_first_out", 2))
            for b in range(2):
                r_group_pe(e, b)
            attention_pe(e)

        def r_group_pe(e, b):
            def prod(bk, left, right):
                for z in range(2):
                    tok = slice(z * P, (z + 1) * P)
                    for m in range(4):
                        ft = 2 * b + m // 2
                        ins = nc.tensor.matmul(bank(bk + m % 2, (2 * z + m // 2) * P, P), left[half(m), ft, tok], right[half(m), ft, tok],
                                               start=True, stop=True)
                return ins
            prod(0, r_al, r_bh)
            prod(2, r_kh, r_al)
            prod(4, r_bh, r_rh)
            prod(6, r_kh, r_rh).then_inc(sems["scores_ready"], e.one("scores_ready"))
            e.eng.wait_ge(sems["r_scores_out"], e.take("r_scores_out"))
            for z in range(2):
                for m in range(4):
                    ins = nc.tensor.transpose(bank(z, m * P, P), r_m[z][:, m, :], ident)
            ins.then_inc(sems["r_turned"], e.one("r_turned"))
            invert_pe(e, r_m, r_tt, r_mb, r_p1)

            def vcols(m):
                return slice((4 * b + m) * 64, (4 * b + m + 1) * 64)
            for z in range(2):
                tok = slice(z * P, (z + 1) * P)
                kw = {"skip_group_check": True}
                for m in range(4):
                    o = bank(6, m * 64, 64)
                    ft = 2 * b + m // 2
                    ins = nc.tensor.matmul(o, r_nt[z][:, m, :], r_v[:, z, vcols(m)], start=True, stop=z == 0)
                    if z:
                        ins = nc.tensor.matmul(o, r_al[:, ft, tok], r_s[:, m, :], start=False, stop=True)
                ins.then_inc(sems["r_rhs_ready"], e.one("r_rhs_ready"))
                e.eng.wait_ge(sems["r_rhs_out"], e.take("r_rhs_out"))
                for m in range(4):
                    ins = nc.tensor.matmul(bank(7, m * 64, 64), r_tt[z][:, m, :], r_rhs[:, m, :], start=True, stop=True)
                ins.then_inc(sems["r_u_ready"], e.one("r_u_ready"))
                e.eng.wait_ge(sems["r_u_out"], e.take("r_u_out"))
                for m in range(4):
                    o = bank(2, m * 64, 64)
                    ft = 2 * b + m // 2
                    nc.tensor.matmul(o, r_rb[z][:, m, :], r_u[:, m, :], start=True, stop=False)
                    ins = nc.tensor.matmul(o, r_rk[z][:, m, :], r_v[:, z, vcols(m)], start=False, stop=z == 0)
                    if z:
                        ins = nc.tensor.matmul(o, r_rh[:, ft, tok], r_s[:, m, :], start=False, stop=True)
                ins.then_inc(sems["r_y_ready"], e.one("r_y_ready"))
                if z == 0:
                    for j in range(2):
                        ft = 2 * b + j
                        nc.tensor.matmul(bank(3, j * P, P), r_bt[:, ft * P:(ft + 1) * P], r_u[:, 2 * j:2 * j + 2, :],
                                         start=True, stop=False)
                        ins = nc.tensor.matmul(bank(3, j * P, P), r_kt[:, ft * P:(ft + 1) * P], r_v[:, 0, ft * P:(ft + 1) * P],
                                               start=False, stop=True)
                    ins.then_inc(sems["r_state_ready"], e.one("r_state_ready"))
                    e.eng.wait_ge(sems["r_state_out"], e.take("r_state_out"))
                e.eng.wait_ge(sems["r_y_out"], e.take("r_y_out"))

        def mixtwo_act(e, l):
            normed_act(e, lambda kb: col("norm_mix_2", kb))
            for j in range(7):
                page_products(e)
                nc.scalar.copy(r_raw[:, 2 * j:2 * j + 2, 1:], bank(j % 2)) \
                    .then_inc(sems["projected_out"], e.one("projected_out"))
            e.mark("r_raw_out", "projected_out")
            for j in range(6):
                page_products(e)
                nc.scalar.copy(d_qkv[:, :, j * 256:(j + 1) * 256], bank(1 - j % 2)) \
                    .then_inc(sems["projected_out"], e.one("projected_out"))
            e.mark("d_qkv_out", "projected_out")
            for j in range(8):
                page_products(e)
                nc.scalar.activation(x_gates[:, :, j * 256:(j + 1) * 256], bank(1 - j % 2), ACT.Sigmoid) \
                    .then_inc(sems["projected_out"], e.one("projected_out"))
            e.mark("x_gates_out", "projected_out")
            e.eng.wait_ge(sems["shifted_ready"], e.take("shifted_ready"))
            nc.scalar.activation(r_x[0:64, 12, :], r_x[0:64, 12, :], ACT.Tanh)
            nc.scalar.activation(r_x[:, 13, :], r_x[:, 13, :], ACT.Sigmoid) \
                .then_inc(sems["lora_in_ready"], e.one("lora_in_ready"))
            e.eng.wait_ge(sems["lora_ready"], e.take("lora_ready"))
            for c in range(4):
                nc.scalar.activation(r_lw[:, c, :], bank(4 + c // 2, (c % 2) * 256, 256), ACT.Sigmoid, bias=col("rwkv_w0_2", c))
                ins = nc.scalar.activation(r_a[:, c, :], bank(6 + c // 2, (c % 2) * 256, 256), ACT.Sigmoid,
                                           bias=col("rwkv_a0_2", c))
            ins.then_inc(sems["r_sigmoids_ready"], e.one("r_sigmoids_ready"))
            e.eng.wait_ge(sems["r_gate_ready"], e.take("r_gate_ready"))
            for t in range(TT):
                ins = nc.scalar.copy(r_gate[:, t, :], bank(t))
            ins.then_inc(sems["r_gate_out"], e.one("r_gate_out"))
            turn_act(e, lambda c: r_v[:, :, c * P:(c + 1) * P], 2)
            e.mark("r_values_turned", "turned_out_act")
            e.eng.wait_ge(sems["square_sums_ready"], e.take("square_sums_ready"))
            nc.scalar.activation(r_t[:, 0, :, :], r_t[:, 0, :, :], ACT.Sqrt) \
                .then_inc(sems["roots_ready"], e.one("roots_ready"))
            e.eng.wait_ge(sems["r_logs_ready"], e.take("r_logs_ready"))
            nc.scalar.activation(r_rh, r_gc, ACT.Exp)
            nc.scalar.activation(r_al, r_lw, ACT.Exp)
            nc.scalar.activation(r_bh, r_gc, ACT.Exp, scale=-1.0) \
                .then_inc(sems["r_exps_ready"], e.one("r_exps_ready"))
            e.eng.wait_ge(sems["r_first_turned"], e.take("r_first_turned"))
            nc.scalar.copy(r_bt, bank(5)).then_inc(sems["r_first_out"], e.one("r_first_out"))
            e.eng.wait_ge(sems["r_first_out"], e.own("r_first_out"))
            nc.scalar.copy(r_kt, bank(6)).then_inc(sems["r_first_out"], e.one("r_first_out"))
            for b in range(2):
                e.eng.wait_ge(sems["r_turned"], e.take("r_turned"))
                for z in range(2):
                    ins = nc.scalar.copy(r_mt[z], quad(bank(z)))
                ins.then_inc(sems["r_turned_out"], e.one("r_turned_out"))
                invert_act(e, r_p1)
                for z in range(2):
                    e.eng.wait_ge(sems["r_rhs_ready"], e.take("r_rhs_ready"))
                    nc.scalar.activation(r_rhs, bank(6, 0, 256).rearrange("p (m s) -> p m s", m=4), ACT.Copy,
                                         scale=-1.0).then_inc(sems["r_rhs_out"], e.one("r_rhs_out"))
                    e.eng.wait_ge(sems["r_u_ready"], e.take("r_u_ready"))
                    nc.scalar.copy(r_u, bank(7, 0, 256).rearrange("p (m s) -> p m s", m=4)) \
                        .then_inc(sems["r_u_out"], e.one("r_u_out"))
                    e.eng.wait_ge(sems["r_y_ready"], e.take("r_y_ready"))
                    nc.scalar.copy(r_y[:, z, b * 256:(b + 1) * 256], bank(2, 0, 256)) \
                        .then_inc(sems["r_y_out"], e.one("r_y_out"))
            e.mark("r_y_done", "r_y_out")
            group_norm_root_act(e, r_root, r_ss, 64, eps=1)
            attention_act(e)

        def mixtwo_dve(e, l):
            nc.vector.memset(r_raw[:, :, 0:1], 0.0).then_inc(sems["vector_step"], e.one("vector_step"))
            normed_dve(e, lambda kb: col("norm_mix_2", kb))
            e.eng.wait_ge(sems["turned_out_dve"], e.own("turned_out_dve"))
            e.page += 21
            e.eng.wait_ge(sems[e.marked("r_raw_out")], e.reach("r_raw_out"))
            for lo, n in ((0, 7), (7, 7)):
                nc.vector.tensor_tensor(r_x[:, lo:lo + n, :], r_raw[:, lo:lo + n, 0:SEQ],
                                        r_raw[:, lo:lo + n, 1:], ALU.subtract) \
                   .then_inc(sems["vector_step"], e.one("vector_step"))
                e.eng.wait_ge(sems["vector_step"], e.own("vector_step"))
            nc.vector.tensor_tensor(r_x, r_x, columns("rwkv_mu_2", 14), ALU.mult) \
               .then_inc(sems["vector_step"], e.one("vector_step"))
            e.eng.wait_ge(sems["vector_step"], e.own("vector_step"))
            nc.vector.tensor_tensor(r_x, r_x, r_raw[:, :, 1:], ALU.add) \
                .then_inc(sems["shifted_ready"], e.one("shifted_ready"))
            e.eng.wait_ge(sems["shifted_ready"], e.own("shifted_ready"))
            r, k = r_x[:, 0:4, :], r_x[:, 4:8, :]
            e.eng.wait_ge(sems[e.marked("x_gates_out")], e.reach("x_gates_out"))
            e.eng.wait_ge(sems["r_sigmoids_ready"], e.take("r_sigmoids_ready"))
            nc.vector.tensor_tensor(r_kk, k, columns("rwkv_k_k_2", 4), ALU.mult) \
               .then_inc(sems["vector_step"], e.one("vector_step"))
            e.eng.wait_ge(sems["vector_step"], e.own("vector_step"))
            nc.vector.tensor_tensor(r_t[:, 0, :, :], r_kk, r_kk, ALU.mult) \
                .then_inc(sems["r_squares_ready"], e.one("r_squares_ready"))
            nc.vector.scalar_tensor_tensor(r_t[:, 1, :, :], r_a, 1.0, columns("rwkv_k_a_2", 4),
                                           ALU.subtract, ALU.mult) \
               .then_inc(sems["vector_step"], e.one("vector_step"))
            e.eng.wait_ge(sems["vector_step"], e.own("vector_step"))
            nc.vector.scalar_tensor_tensor(k, r_t[:, 1, :, :], 1.0, k, ALU.add, ALU.mult) \
               .then_inc(sems["vector_step"], e.one("vector_step"))
            e.eng.wait_ge(sems["vector_step"], e.own("vector_step"))
            nc.vector.tensor_tensor(r_t[:, 1, :, :], r, k, ALU.mult).then_inc(sems["vector_step"], e.one("vector_step"))
            e.eng.wait_ge(sems["vector_step"], e.own("vector_step"))
            nc.vector.tensor_tensor(r_t[:, 1, :, :], r_t[:, 1, :, :], columns("rwkv_r_k_2", 4), ALU.mult) \
                .then_inc(sems["r_bonus_in_ready"], e.one("r_bonus_in_ready"))
            e.eng.wait_ge(sems["r_norm_ready"], e.take("r_norm_ready"))
            for b in range(2):
                ins = nc.vector.tensor_scalar(r_t[:, 0, 2 * b:2 * b + 2, :],
                                              bank(b).rearrange("p (c s) -> p c s", c=2), 1.0e-24, None, ALU.max)
            ins.then_inc(sems["square_sums_ready"], e.one("square_sums_ready"))
            turn_dve(e, lambda c: r_v[:, :, c * P:(c + 1) * P], 2)
            nc.vector.tensor_scalar(r_lw, r_lw, -RC, None, ALU.mult).then_inc(sems["vector_step"], e.one("vector_step"))
            e.eng.wait_ge(sems["vector_step"], e.own("vector_step"))
            for c in range(4):
                ins = nc.vector.tensor_tensor_scan(r_gc[:, c, :], const("restart128"), r_lw[:, c, :], 0.0,
                                                   ALU.mult, ALU.add)
            ins.then_inc(sems["vector_step"], e.one("vector_step"))
            e.eng.wait_ge(sems["vector_step"], e.own("vector_step"))
            nc.vector.tensor_tensor(r_lw, r_gc, r_lw, ALU.subtract) \
                .then_inc(sems["r_logs_ready"], e.one("r_logs_ready"))
            e.eng.wait_ge(sems["roots_ready"], e.take("roots_ready"))
            nc.vector.reciprocal(r_t[:, 0, :, :], r_t[:, 0, :, :]).then_inc(sems["vector_step"], e.one("vector_step"))
            e.eng.wait_ge(sems["vector_step"], e.own("vector_step"))
            nc.vector.tensor_tensor(r_kk, r_kk, r_t[:, 0, :, :], ALU.mult) \
               .then_inc(sems["vector_step"], e.one("vector_step"))
            e.eng.wait_ge(sems["vector_step"], e.own("vector_step"))
            e.eng.wait_ge(sems["r_exps_ready"], e.take("r_exps_ready"))
            nc.vector.tensor_copy(r_end, r_rh[:, :, P - 1]).then_inc(sems["vector_step"], e.one("vector_step"))
            e.eng.wait_ge(sems["vector_step"], e.own("vector_step"))
            nc.vector.tensor_tensor(r_rh, r_rh, r, ALU.mult)
            nc.vector.tensor_tensor(r_al, r_al, r_kk, ALU.mult)
            nc.vector.tensor_tensor(r_kh, r_bh, k, ALU.mult)
            nc.vector.tensor_tensor(r_a, r_a, r_kk, ALU.mult).then_inc(sems["vector_step"], e.one("vector_step"))
            e.eng.wait_ge(sems["vector_step"], e.own("vector_step"))
            nc.vector.tensor_tensor(r_bh, r_bh, r_a, ALU.mult).then_inc(sems["vector_step"], e.one("vector_step"))
            e.eng.wait_ge(sems["vector_step"], e.own("vector_step"))
            e.eng.wait_ge(sems["r_bonus_ready"], e.take("r_bonus_ready"))
            nc.vector.tensor_copy(r_bonus, bank(4, 0, 32).rearrange("p (t n) -> p t n", t=TT)[:, :, 0:8]) \
                .then_inc(sems["r_factors_ready"], e.one("r_factors_ready"))
            for b in range(2):
                e.eng.wait_ge(sems["scores_ready"], e.take("scores_ready"))
                for z in range(2):
                    for dst, bk, mask in ((r_m, 0, const("after")), (r_nt, 2, const("before")), (r_rb, 4, upto), (r_rk, 6, upto)):
                        for o in range(2):
                            ins = nc.vector.tensor_tensor(dst[z][:, o::2, :],
                                                          bank(bk + o, z * 256, 256).rearrange("p (m s) -> p m s", m=2),
                                                          mask.unsqueeze(1).to_broadcast([P, 2, P]), ALU.mult)
                ins.then_inc(sems["r_scores_out"], e.one("r_scores_out"))
                e.eng.wait_ge(sems["r_scores_out"], e.own("r_scores_out"))
                e.eng.wait_ge(sems["r_turned_out"], e.take("r_turned_out"))
                invert_dve(e, r_m, r_tt, r_mt, r_mb)
                nc.vector.memset(r_s, 0.0).then_inc(sems["vector_step"], e.one("vector_step"))
                e.eng.wait_ge(sems["vector_step"], e.own("vector_step"))
                e.eng.wait_ge(sems["r_state_ready"], e.take("r_state_ready"))
                for m in range(4):
                    ft, h = 2 * b + m // 2, half(m)
                    ins = nc.vector.tensor_scalar(r_s[h, m, :], bank(3, (m // 2) * P + (m % 2) * 64, 64)[h, :],
                                                  r_end[h, ft:ft + 1], None, ALU.mult)
                ins.then_inc(sems["r_state_out"], e.one("r_state_out"))
            e.eng.wait_ge(sems[e.marked("r_y_done")], e.reach("r_y_done"))
            e.eng.wait_ge(sems[e.marked("r_values_turned")], e.reach("r_values_turned"))
            sq = flat(hflat, 1024, TT, RW)

            def by_head(ap):
                return ap.rearrange("p t (h n) -> p (t h) n", n=64)

            def each(s):
                return s.rearrange("p t h -> p (t h)").unsqueeze(2).to_broadcast([P, 16, 64])
            nc.vector.tensor_reduce(r_mean.rearrange("p t h -> p (t h)"), by_head(r_y), AX.X, ALU.add) \
               .then_inc(sems["vector_step"], e.one("vector_step"))
            e.eng.wait_ge(sems["vector_step"], e.own("vector_step"))
            nc.vector.tensor_scalar(r_mean, r_mean, 1.0 / 64, None, ALU.mult) \
               .then_inc(sems["vector_step"], e.one("vector_step"))
            e.eng.wait_ge(sems["vector_step"], e.own("vector_step"))
            nc.vector.tensor_tensor(by_head(r_y), by_head(r_y), each(r_mean), ALU.subtract) \
               .then_inc(sems["vector_step"], e.one("vector_step"))
            e.eng.wait_ge(sems["vector_step"], e.own("vector_step"))
            nc.vector.tensor_tensor(sq, r_y, r_y, ALU.mult).then_inc(sems["vector_step"], e.one("vector_step"))
            e.eng.wait_ge(sems["vector_step"], e.own("vector_step"))
            nc.vector.tensor_reduce(r_ss.rearrange("p t h -> p (t h)"), by_head(sq), AX.X, ALU.add) \
                .then_inc(sems["square_sums_ready"], e.one("square_sums_ready"))
            e.eng.wait_ge(sems["roots_ready"], e.take("roots_ready"))
            nc.vector.reciprocal(r_rec, r_root).then_inc(sems["vector_step"], e.one("vector_step"))
            e.eng.wait_ge(sems["vector_step"], e.own("vector_step"))
            nc.vector.tensor_tensor(by_head(r_y), by_head(r_y), each(r_rec), ALU.mult) \
               .then_inc(sems["vector_step"], e.one("vector_step"))
            e.eng.wait_ge(sems["vector_step"], e.own("vector_step"))
            nc.vector.tensor_tensor(r_y, r_y, row("rwkv_ln_w_2").unsqueeze(1).to_broadcast([P, TT, RW]), ALU.mult) \
               .then_inc(sems["vector_step"], e.one("vector_step"))
            e.eng.wait_ge(sems["vector_step"], e.own("vector_step"))
            nc.vector.tensor_tensor(r_y, r_y, row("rwkv_ln_b_2").unsqueeze(1).to_broadcast([P, TT, RW]), ALU.add) \
               .then_inc(sems["vector_step"], e.one("vector_step"))
            e.eng.wait_ge(sems["vector_step"], e.own("vector_step"))
            nc.vector.tensor_tensor(by_head(sq), by_head(r_v), each(r_bonus), ALU.mult) \
               .then_inc(sems["vector_step"], e.one("vector_step"))
            e.eng.wait_ge(sems["vector_step"], e.own("vector_step"))
            nc.vector.tensor_tensor(r_y, r_y, sq, ALU.add).then_inc(sems["vector_step"], e.one("vector_step"))
            e.eng.wait_ge(sems["vector_step"], e.own("vector_step"))
            nc.vector.tensor_tensor(r_y, r_y, r_gate, ALU.mult).then_inc(sems["vector_step"], e.one("vector_step"))
            e.eng.wait_ge(sems["vector_step"], e.own("vector_step"))
            attention_dve(e)

        LAM_INIT = 0.2
        d_sq = flat(bufA, 0, TT, 1024)
        d_rot = flat(bufA, 2048, TT, 1024)
        d_qT, d_kT = flat(bufA, 4096, 4, SEQ), flat(bufA, 5120, 4, SEQ)
        d_p = flat(bufA, 0, 4, 2, 384)
        d_pT = flat(bufA, 6144, 4, 384)
        d_o = flat(bufE, 0, TT, RW)
        d_ss, d_root, d_rec = (s2(216 + 32 * k, 16) for k in range(3))
        d_max = st[:, 320:336].rearrange("p (h c t) -> p h c t", h=4, c=2)
        d_sum = st[:, 336:352].rearrange("p (h c t) -> p h c t", h=4, c=2)
        d_lam = st[:, 352:360]
        d_oss, d_oroot, d_orec = (s2(360 + 8 * k, 4) for k in range(3))
        x_mix = flat(bufC, 0, TT, D)

        def attention_pe(e):
            e.eng.wait_ge(sems["rotated_ready"], e.take("rotated_ready"))
            for g in range(4):
                if g >= 2:
                    done = ("turned_out_act", "turned_out_dve")[g % 2]
                    e.eng.wait_ge(sems[done], e.take(done))
                for j in range(2):
                    for t in range(TT):
                        at = (g // 2) * RW + (2 * (g % 2) + j) * P
                        ins = nc.tensor.transpose(bank(2 + g % 2, (2 * j + t) * P, P), d_qkv[:, t, at:at + P], ident)
                done = ("turned_act", "turned_dve")[g % 2]
                ins.then_inc(sems[done], e.one(done))
            e.eng.wait_ge(sems["turned_out_act"], e.take("turned_out_act"))
            e.eng.wait_ge(sems["turned_out_dve"], e.take("turned_out_dve"))
            for h in range(4):
                for c in range(2):
                    s = slice(c * 64, c * 64 + 64)
                    if h >= 2:
                        e.eng.wait_ge(sems["d_scores_read"], e.take("d_scores_read"))
                    b = 4 + (2 * h + c) % 4
                    nc.tensor.matmul(bank(b, 0, P), d_qT[s, h, 0:P], d_kT[s, h, 0:P], start=True, stop=True)
                    nc.tensor.matmul(bank(b, P, 256), d_qT[s, h, P:], d_kT[s, h, :], start=True, stop=True) \
                        .then_inc(sems["scores_ready"], e.one("scores_ready"))
            e.eng.wait_ge(sems["d_scores_read"], e.take("d_scores_read", 4))
            for h in range(4):
                e.eng.wait_ge(sems["d_attn_ready"], e.take("d_attn_ready"))
                if h >= 2:
                    e.eng.wait_ge(sems["d_turned_out"], e.take("d_turned_out"))
                for k in range(3):
                    ins = nc.tensor.transpose(bank(h % 2, k * P, P), d_p[:, h, 0, k * P:(k + 1) * P], ident)
                ins.then_inc(sems["d_turned"], e.one("d_turned"))
            for h in range(4):
                if h < 2:
                    e.eng.wait_ge(sems["d_turned_out"], e.take("d_turned_out"))
                v = slice(2 * RW + h * P, 2 * RW + (h + 1) * P)
                if h == 0:
                    e.eng.wait_ge(sems["d_turned_out"], e.ahead("d_turned_out", 1))
                nc.tensor.matmul(bank(4, h * P, P), d_pT[:, h, 0:P], d_qkv[:, 0, v], start=True, stop=True)
                nc.tensor.matmul(bank(5, h * P, P), d_pT[:, h, P:256], d_qkv[:, 0, v], start=True, stop=False)
                ins = nc.tensor.matmul(bank(5, h * P, P), d_pT[:, h, 256:], d_qkv[:, 1, v], start=False, stop=True)
            ins.then_inc(sems["d_out_ready"], e.one("d_out_ready"))
            e.eng.wait_ge(sems["branches_ready"], e.take("branches_ready"))
            for g in range(4):
                src = (r_y, d_o)[g // 2]
                if g >= 2:
                    done = ("turned_out_act", "turned_out_dve")[g % 2]
                    e.eng.wait_ge(sems[done], e.take(done))
                for j in range(2):
                    for t in range(TT):
                        at = (2 * (g % 2) + j) * P
                        ins = nc.tensor.transpose(bank(2 + g % 2, (2 * j + t) * P, P), src[:, t, at:at + P], ident)
                done = ("turned_act", "turned_dve")[g % 2]
                ins.then_inc(sems[done], e.one(done))
            e.eng.wait_ge(sems["turned_out_act"], e.take("turned_out_act"))
            e.eng.wait_ge(sems["turned_out_dve"], e.take("turned_out_dve"))
            for j in range(2):
                page_deep(e, lambda k: yT[:, 2 * j + k, :], j == 0, j == 1, b=4)
            for j in range(2):
                page_deep(e, lambda k: yT[:, 4 + 2 * j + k, :], j == 0, j == 1, b=0)
            e.eng.wait_ge(sems["mixed_ready"], e.take("mixed_ready"))
            turn_pe(e, lambda kb, t: x_mix[:, t, kb * P:(kb + 1) * P], 4)
            down_pe(e, 4, lambda kb: hT[:, kb, :])

        def attention_act(e):
            e.eng.wait_ge(sems["square_sums_ready"], e.take("square_sums_ready"))
            nc.scalar.activation(d_root, d_ss, ACT.Sqrt, bias=const("eps", 0, 1), scale=1.0 / 64) \
                .then_inc(sems["roots_ready"], e.one("roots_ready"))
            for g in (0, 2):
                e.eng.wait_ge(sems["turned_act"], e.take("turned_act"))
                dst = (d_qT, d_kT)[g // 2]
                nc.scalar.copy(dst[:, 0:2, :], bank(2)).then_inc(sems["turned_out_act"], e.one("turned_out_act"))
            e.eng.wait_ge(sems["exponent_ready"], e.take("exponent_ready"))
            nc.scalar.activation(d_lam[:, 2:4], d_lam[:, 0:2], ACT.Exp) \
                .then_inc(sems["exponential_ready"], e.one("exponential_ready"))
            for h in range(4):
                for c in range(2):
                    e.eng.wait_ge(sems["d_max_ready"], e.take("d_max_ready"))
                    for t, s in ((0, slice(0, P)), (1, slice(P, 384))):
                        ins = nc.scalar.activation(d_p[:, h, c, s], d_p[:, h, c, s], ACT.Exp, bias=d_max[:, h, c, t:t + 1],
                                                   scale=0.125, accum_out=d_sum[:, h, c, t:t + 1])
                    ins.then_inc(sems["d_exp_ready"], e.one("d_exp_ready"))
            for h in range(4):
                e.eng.wait_ge(sems["d_turned"], e.take("d_turned"))
                nc.scalar.copy(d_pT[:, h, :], bank(h % 2, 0, 384)) \
                    .then_inc(sems["d_turned_out"], e.one("d_turned_out"))
            e.eng.wait_ge(sems["d_out_ready"], e.take("d_out_ready"))
            for t in range(TT):
                ins = nc.scalar.copy(d_o[:, t, :], bank(4 + t))
            ins.then_inc(sems["d_out_copied"], e.one("d_out_copied"))
            e.eng.wait_ge(sems["square_sums_ready"], e.take("square_sums_ready"))
            nc.scalar.activation(d_oroot, d_oss, ACT.Sqrt, bias=const("eps", 0, 1), scale=1.0 / P) \
                .then_inc(sems["roots_ready"], e.one("roots_ready"))
            for g in (0, 2):
                e.eng.wait_ge(sems["turned_act"], e.take("turned_act"))
                for j in range(2):
                    ins = nc.scalar.activation(yT[:, 2 * g + j, :], bank(2, j * 256, 256), ACT.Copy,
                                               scale=1.0 if g == 0 else col("subln_w_2", 0))
                ins.then_inc(sems["turned_out_act"], e.one("turned_out_act"))
            e.page += 4
            turn_act(e, lambda kb: hT[:, kb, :], 4)
            e.page += 4

        def attention_dve(e):
            e.eng.wait_ge(sems[e.marked("d_qkv_out")], e.reach("d_qkv_out"))
            def heads16(ap):
                return ap.rearrange("p (g n) -> p g n", n=64)
            for t in range(TT):
                ins = nc.vector.tensor_tensor(d_sq[:, t, :], d_qkv[:, t, 0:1024], d_qkv[:, t, 0:1024], ALU.mult)
            ins.then_inc(sems["vector_step"], e.one("vector_step"))
            e.eng.wait_ge(sems["vector_step"], e.own("vector_step"))
            for t in range(TT):
                ins = nc.vector.tensor_reduce(d_ss[:, t, :], heads16(d_sq[:, t, :]), AX.X, ALU.add)
            ins.then_inc(sems["square_sums_ready"], e.one("square_sums_ready"))
            e.eng.wait_ge(sems["roots_ready"], e.take("roots_ready"))
            nc.vector.reciprocal(d_rec, d_root).then_inc(sems["vector_step"], e.one("vector_step"))
            e.eng.wait_ge(sems["vector_step"], e.own("vector_step"))
            for t in range(TT):
                v = heads16(d_qkv[:, t, 0:1024])
                ins = nc.vector.tensor_tensor(v, v, d_rec[:, t, :].unsqueeze(2).to_broadcast([P, 16, 64]), ALU.mult)
            ins.then_inc(sems["vector_step"], e.one("vector_step"))
            e.eng.wait_ge(sems["vector_step"], e.own("vector_step"))
            for t in range(TT):
                for lo, gain in ((0, "q_norm_2"), (RW, "k_norm_2")):
                    v = heads16(d_qkv[:, t, lo:lo + RW])
                    ins = nc.vector.tensor_tensor(v, v, row(gain).unsqueeze(1).to_broadcast([P, 8, 64]), ALU.mult)
            ins.then_inc(sems["vector_step"], e.one("vector_step"))
            e.eng.wait_ge(sems["vector_step"], e.own("vector_step"))
            for t in range(TT):
                v, o = heads16(d_qkv[:, t, 0:1024]), heads16(d_rot[:, t, :])
                sin = const("sin", 64 * t, 64).unsqueeze(1).to_broadcast([P, 16, 64])
                nc.vector.tensor_tensor(o[:, :, 0:32], v[:, :, 32:64], sin[:, :, 0:32], ALU.mult)
                ins = nc.vector.tensor_tensor(o[:, :, 32:64], v[:, :, 0:32], sin[:, :, 32:64], ALU.mult)
            ins.then_inc(sems["vector_step"], e.one("vector_step"))
            e.eng.wait_ge(sems["vector_step"], e.own("vector_step"))
            for t in range(TT):
                v = heads16(d_qkv[:, t, 0:1024])
                ins = nc.vector.tensor_tensor(v, v, const("cos", 64 * t, 64).unsqueeze(1).to_broadcast([P, 16, 64]), ALU.mult)
            ins.then_inc(sems["vector_step"], e.one("vector_step"))
            e.eng.wait_ge(sems["vector_step"], e.own("vector_step"))
            for t in range(TT):
                v = d_qkv[:, t, 0:1024]
                ins = nc.vector.tensor_tensor(v, v, d_rot[:, t, :], ALU.add)
            ins.then_inc(sems["rotated_ready"], e.one("rotated_ready"))
            for g in (1, 3):
                e.eng.wait_ge(sems["turned_dve"], e.take("turned_dve"))
                dst = (d_qT, d_kT)[g // 2]
                nc.vector.tensor_copy(dst[:, 2:4, :], bank(3).rearrange("p (c s) -> p c s", c=2)) \
                    .then_inc(sems["turned_out_dve"], e.one("turned_out_dve"))
            for i, (a, b) in enumerate((("lambda_q1_2", "lambda_k1_2"), ("lambda_q2_2", "lambda_k2_2"))):
                ins = nc.vector.tensor_tensor(st[:, 400 + 64 * i:464 + 64 * i], row(a), row(b), ALU.mult)
            ins.then_inc(sems["vector_step"], e.one("vector_step"))
            e.eng.wait_ge(sems["vector_step"], e.own("vector_step"))
            nc.vector.tensor_reduce(d_lam[:, 0:2], st[:, 400:528].rearrange("p (i n) -> p i n", i=2), AX.X, ALU.add) \
                .then_inc(sems["exponent_ready"], e.one("exponent_ready"))
            e.eng.wait_ge(sems["exponential_ready"], e.take("exponential_ready"))
            nc.vector.tensor_tensor(d_lam[:, 4:5], d_lam[:, 3:4], d_lam[:, 2:3], ALU.subtract) \
               .then_inc(sems["vector_step"], e.one("vector_step"))
            e.eng.wait_ge(sems["vector_step"], e.own("vector_step"))
            nc.vector.tensor_scalar(d_lam[:, 4:5], d_lam[:, 4:5], LAM_INIT, None, ALU.subtract) \
               .then_inc(sems["vector_step"], e.one("vector_step"))
            e.eng.wait_ge(sems["vector_step"], e.own("vector_step"))
            for h in range(4):
                for c in range(2):
                    e.eng.wait_ge(sems["scores_ready"], e.take("scores_ready"))
                    p = d_p[:, h, c, :]
                    nc.vector.tensor_tensor(p, bank(4 + (2 * h + c) % 4, 0, 384), const("causal3"), ALU.add) \
                        .then_inc(sems["d_scores_read"], e.one("d_scores_read"))
                    e.eng.wait_ge(sems["d_scores_read"], e.own("d_scores_read"))
                    nc.vector.tensor_reduce(d_max[:, h, c, 0:1], p[:, 0:P], AX.X, ALU.max)
                    nc.vector.tensor_reduce(d_max[:, h, c, 1:2], p[:, P:384], AX.X, ALU.max) \
                       .then_inc(sems["vector_step"], e.one("vector_step"))
                    e.eng.wait_ge(sems["vector_step"], e.own("vector_step"))
                    nc.vector.tensor_scalar(d_max[:, h, c, :], d_max[:, h, c, :], -0.125, None, ALU.mult) \
                        .then_inc(sems["d_max_ready"], e.one("d_max_ready"))
            e.eng.wait_ge(sems["d_exp_ready"], e.take("d_exp_ready", 8))
            nc.vector.reciprocal(st[:, 336:352], st[:, 336:352]).then_inc(sems["vector_step"], e.one("vector_step"))
            e.eng.wait_ge(sems["vector_step"], e.own("vector_step"))
            nc.vector.tensor_tensor(d_sum[:, :, 1, :], d_sum[:, :, 1, :],
                                    d_lam[:, 4:5].unsqueeze(2).to_broadcast([P, 4, 2]), ALU.mult) \
               .then_inc(sems["vector_step"], e.one("vector_step"))
            e.eng.wait_ge(sems["vector_step"], e.own("vector_step"))
            for h in range(4):
                for t, s in ((0, slice(0, P)), (1, slice(P, 384))):
                    ins = nc.vector.tensor_scalar(d_p[:, h, 0, s], d_p[:, h, 0, s], d_sum[:, h, 0, t:t + 1], None, ALU.mult)
                ins.then_inc(sems["vector_step"], e.one("vector_step"))
                e.eng.wait_ge(sems["vector_step"], e.own("vector_step"))
                for t, s in ((0, slice(0, P)), (1, slice(P, 384))):
                    ins = nc.vector.scalar_tensor_tensor(d_p[:, h, 0, s], d_p[:, h, 1, s], d_sum[:, h, 1, t:t + 1],
                                                         d_p[:, h, 0, s], ALU.mult, ALU.add)
                ins.then_inc(sems["d_attn_ready"], e.one("d_attn_ready"))
            e.eng.wait_ge(sems["d_out_copied"], e.take("d_out_copied"))
            nc.vector.tensor_tensor(d_sq[:, :, 0:RW], d_o, d_o, ALU.mult) \
               .then_inc(sems["vector_step"], e.one("vector_step"))
            e.eng.wait_ge(sems["vector_step"], e.own("vector_step"))
            for t in range(TT):
                ins = nc.vector.tensor_reduce(d_oss[:, t, :], d_sq[:, t, 0:RW].rearrange("p (g n) -> p g n", n=P),
                                              AX.X, ALU.add)
            ins.then_inc(sems["square_sums_ready"], e.one("square_sums_ready"))
            e.eng.wait_ge(sems["roots_ready"], e.take("roots_ready"))
            nc.vector.reciprocal(d_orec, d_oroot).then_inc(sems["vector_step"], e.one("vector_step"))
            e.eng.wait_ge(sems["vector_step"], e.own("vector_step"))
            nc.vector.tensor_scalar(d_orec, d_orec, 1.0 - LAM_INIT, None, ALU.mult) \
               .then_inc(sems["vector_step"], e.one("vector_step"))
            e.eng.wait_ge(sems["vector_step"], e.own("vector_step"))
            for t in range(TT):
                v = d_o[:, t, :].rearrange("p (g n) -> p g n", n=P)
                ins = nc.vector.tensor_tensor(v, v, d_orec[:, t, :].unsqueeze(2).to_broadcast([P, 4, P]), ALU.mult)
            ins.then_inc(sems["branches_ready"], e.one("branches_ready"))
            for g in (1, 3):
                e.eng.wait_ge(sems["turned_dve"], e.take("turned_dve"))
                for j in range(2):
                    c = 2 * g + j
                    gain = 1.0 if g == 1 else col("subln_w_2", 0)
                    ins = nc.vector.tensor_scalar(yT[:, (2, 6)[g // 2] + j, :], bank(3, j * 256, 256), gain, None, ALU.mult)
                ins.then_inc(sems["turned_out_dve"], e.one("turned_out_dve"))
            e.eng.wait_ge(sems[e.marked("x_gates_out")], e.reach("x_gates_out"))
            page_products(e, 2)
            for t in range(TT):
                for k in range(2):
                    s = slice(k * 512, (k + 1) * 512)
                    ins = nc.vector.tensor_tensor(x_mix[:, t, s], x_gates[:, t, s], bank(4 + 2 * t + k), ALU.mult)
            ins.then_inc(sems["vector_step"], e.one("vector_step"))
            e.eng.wait_ge(sems["vector_step"], e.own("vector_step"))
            page_products(e, 2)
            for t in range(TT):
                for k in range(2):
                    s = slice(k * 512, (k + 1) * 512)
                    w = x_gates[:, t, D + k * 512:D + (k + 1) * 512]
                    ins = nc.vector.tensor_tensor(w, w, bank(2 * t + k), ALU.mult)
            ins.then_inc(sems["vector_step"], e.one("vector_step"))
            e.eng.wait_ge(sems["vector_step"], e.own("vector_step"))
            nc.vector.tensor_tensor(x_mix, x_mix, x_gates[:, :, D:], ALU.add) \
                .then_inc(sems["mixed_ready"], e.one("mixed_ready"))
            turn_dve(e, lambda kb: hT[:, kb, :], 4)
            residual_dve(e, 4)

        stages = {
            "xattn": (xattn_pe, xattn_act, xattn_dve),
            "ffn": (ffn_pe, ffn_act, ffn_dve),
            "final": (None, lambda e, l: final_act(e), lambda e, l: final_dve(e)),
            "moe": (lambda e, l: moe_pe(e), lambda e, l: moe_act(e), lambda e, l: moe_dve(e)),
            "ple": (lambda e, l: ple_pe(e), lambda e, l: ple_act(e), lambda e, l: ple_dve(e)),
            "mamba": (mamba_pe, mamba_act, mamba_dve),
            "hgrn": (hgrn_pe, hgrn_act, hgrn_dve),
            "gdn": (gdn_pe, gdn_act, gdn_dve),
            "mixtwo": (mixtwo_pe, mixtwo_act, mixtwo_dve),
        }

        block = ctx.enter_context(nc.Block())

        @block.sync
        def _(sp):
            def load(page, slot):
                sp.dma_start(ring[:, slot, :], pages_in[bass.ds(page, 1)].rearrange("a p n -> (a p) n")) \
                    .then_inc(sems[f"page_landed_{slot}"], 16)

            sp.dma_start(mem, mem_in).then_inc(sems["memory_loaded"], 16)
            sp.dma_start(consts[:, :], consts_in).then_inc(sems["constants_loaded"], 16)
            sp.dma_start(cols[:, :], cols_in).then_inc(sems["constants_loaded"], 16)
            sp.dma_start(x[:, :, :], x_in).then_inc(sems["x_loaded"], 16)
            load(0, 0)
            sp.dma_start(smalls[:, :], smalls_in).then_inc(sems["tables_loaded"], 16)
            sp.dma_start(rows[:, :], rows_in.to_broadcast([P, N_ROWS])).then_inc(sems["tables_loaded"], 16)
            for s in range(1, RING):
                load(s, s)
            rounds = total_pages // RING - 1
            with sp.Fori(0, rounds) as i:
                for s in range(RING):
                    sp.wait_ge(sems["page_done"], i * RING + s + 1)
                    load(i * RING + RING + s, s)
            for s in range(total_pages % RING):
                page = (rounds + 1) * RING + s
                sp.wait_ge(sems["page_done"], page - RING + 1)
                load(page, s)
            sp.wait_ge(sems["x_ready"], 1 + len(PLAN))
            sp.dma_start(out, x[:, :, :]).then_inc(sems["out_stored"], 16)
            sp.wait_ge(sems["out_stored"], 16)

        @block.gpsimd
        def _(pool):
            pass

        @block.tensor
        def _(pe):
            e = Program(pe, sems, "tensor")
            pe.wait_ge(sems["constants_loaded"], 32)
            e.eng.wait_ge(sems["normed_ready"], e.take("normed_ready", 2))
            turn_pe(e, lambda kb, t: xn[:, t, kb * P:(kb + 1) * P], KB // 2)
            pe.wait_ge(sems["tables_loaded"], 32)
            for s in PLAN:
                kind, l = split_stage(s)
                if stages[kind][0]:
                    stages[kind][0](e, l)

        @block.scalar
        def _(act):
            e = Program(act, sems, "scalar")
            act.wait_ge(sems["constants_loaded"], 32)
            for k in range(2):
                nc.scalar.copy(st[:, 110 + k:111 + k], ones[:, 0:1]) \
                    .then_inc(sems["projected_out"], e.one("projected_out"))
            memory_act(e)
            act.wait_ge(sems["tables_loaded"], 32)
            for s in PLAN:
                kind, l = split_stage(s)
                stages[kind][1](e, l)

        @block.vector
        def _(dve):
            e = Program(dve, sems, "vector")
            dve.wait_ge(sems["constants_loaded"], 32)
            memory_dve(e)
            dve.wait_ge(sems["turned_out_act"], 2)
            dve.wait_ge(sems["x_loaded"], 16)
            dve.wait_ge(sems["tables_loaded"], 32)
            nc.vector.memset(st[:, 112:113], 0.0).then_inc(sems["x_ready"], e.one("x_ready"))
            if split_stage(PLAN[0])[0] == "xattn":
                xattn_open_dve(e, split_stage(PLAN[0])[1])
            for s, after in zip(PLAN, PLAN[1:] + [None]):
                kind, l = split_stage(s)
                e.next_stage = after
                stages[kind][2](e, l)


def wide(w, n0, n=256):
    return w[:, n0:n0 + n].reshape(KB, P, n).transpose(1, 0, 2).reshape(P, -1)


def deep(w, j):
    return w[256 * j:256 * j + 256].reshape(2, P, D).transpose(1, 0, 2).reshape(P, -1)


def glu_pages(chunks):
    gate, up, down = chunks[0]
    yield gate()
    yield up()
    for c in range(1, len(chunks)):
        yield chunks[c][0]()
        yield chunks[c][1]()
        yield chunks[c - 1][2]()
    yield chunks[-1][2]()


def weight_pages(w):
    for s in PLAN:
        kind, l = split_stage(s)
        if kind == "mamba":
            a = l // 3
            order = list(range(8, 24)) + list(range(8))
            yield from (wide(w["m_in_w"][a], 256 * j) for j in order)
            yield from (deep(w["m_out_w"][a], j) for j in range(8))
        elif kind == "hgrn":
            order = [4, 5, 6, 7, 0, 1, 2, 3, 12, 13, 14, 15, 8, 9, 10, 11]
            yield from (wide(w["h_in_w"][0], 256 * j) for j in order)
            yield from (deep(w["h_out_w"][0], j) for j in range(4))
        elif kind == "gdn":
            yield from (wide(w["g_in_w"][0], 256 * j) for j in range(24))
            yield from (deep(w["g_out_w"][0], j) for j in range(8))
        elif kind == "xattn":
            yield from (wide(w["xa_kv"][l], 256 * j) for j in range(8))
            yield from (wide(w["xa_q"][l], 256 * j) for j in range(4))
            yield from (deep(w["xa_o"][l], j) for j in range(4))
        elif kind == "ffn":
            up, down = w["f_up"][l], w["f_down"][l]
            yield from glu_pages([(lambda c=c: wide(up, 256 * c), lambda c=c: wide(up, D_FF + 256 * c),
                                   lambda c=c: deep(down, c)) for c in range(FFN_CHUNKS)])
        elif kind == "mixtwo":
            yield from (wide(w["w_in_2"][0], 256 * j) for j in range(21))
            yield from (deep(w["w_branch_rwkv_2"][0], j) for j in range(2))
            yield from (deep(w["w_branch_diff_2"][0], j) for j in range(2))
            yield from (deep(w["w_out_2"][0], j) for j in range(4))
        elif kind == "moe":
            g, u, d = w["w_gate_2"][0], w["w_up_2"][0], w["w_down_2"][0]
            yield from glu_pages([(lambda x=x, h=h: wide(g[x], 256 * h), lambda x=x, h=h: wide(u[x], 256 * h),
                                   lambda x=x, h=h: deep(d[x], h)) for x in range(EXPERTS) for h in range(2)])
        elif kind == "ple":
            yield deep(w["w_ple_proj_2"][0], 0)
            yield from (deep(w["w_ple_gate_2"][0], j) for j in range(4))


def kernel(**inputs):
    import numpy as _np
    import concourse.bacc as _bacc
    from concourse import mybir as _mybir
    from concourse.bass_utils import run_bass_kernel_spmd as _run

    w = {k: _np.asarray(v) for k, v in inputs.items()}
    total = sum(pages_of(s) for s in PLAN)
    pages = _np.empty((total, P, PAGE), _np.float32)
    for n, page in enumerate(weight_pages(w)):
        pages[n] = page

    def tokens(a):
        return _np.ascontiguousarray(a.reshape(TT, P, -1).transpose(1, 0, 2))

    cols = _np.concatenate([w[name].reshape(-1, P).T for name, _ in COLS], 1)
    rows = _np.concatenate([w[name].reshape(-1) for name, _ in ROWS])[None, :]
    narrow = [wide(w["m_in_w"][a], 6144, 32) for a in range(2)]
    narrow.append(wide(w["g_in_w"][0], 6144, 32))
    narrow.append(wide(_np.concatenate([w["w_group_2"][0], w["w_expert_router_2"][0]], 1), 0, 36))
    narrow.append(_np.concatenate([w["rwkv_w2_2"][0], w["rwkv_a2_2"][0]], 0))
    narrow.append(w["rwkv_g2_2"][0])
    arrays = {
        "x_dram": tokens(w["x"][0]), "mem_dram": tokens(w["mem"][0]), "p_dram": tokens(w["p_2"][0, 0]),
        "pages_dram": pages, "consts_dram": CONSTS, "cols_dram": _np.ascontiguousarray(cols),
        "rows_dram": _np.ascontiguousarray(rows), "smalls_dram": _np.concatenate(narrow, 1),
        "final_dram": w["final_norm"][None, :],
    }
    nc = _bacc.Bacc("TRN2", target_bir_lowering=False, num_devices=1)
    aps = [nc.dram_tensor(n, a.shape, _mybir.dt.from_np(a.dtype), kind="ExternalInput").ap() for n, a in arrays.items()]
    out = nc.dram_tensor("out_dram", (P, TT, D), F32, kind="ExternalOutput").ap()
    build(nc, *aps, out)
    r = _run(nc, [arrays], core_ids=[0])
    got = _np.asarray(r.results[0]["out_dram"])
    return _np.ascontiguousarray(got.transpose(1, 0, 2)).reshape(1, SEQ, D)
```
